# Optimizing a Trainium2 kernel written in Bass

```python
import jax, jax.numpy as jnp
from jax import lax
import numpy as np

D_MODEL = 2048
BATCH = 1
SEQ = 256
DEPTH = 1

ATTN_HEADS = 8
ATTN_HEAD_DIM = 128
ATTN_WIDTH = ATTN_HEADS * ATTN_HEAD_DIM
DILATED_PATTERNS = ((128, 1), (512, 4), (2048, 16))
Q_BLOCK = 128
ROPE_THETA = 500000.0
ROT_DIM = ATTN_HEAD_DIM // 4
HGRN_HEADS = 8
HGRN_EXPAND = 128
HGRN_HEAD_V = 128
HGRN_KEY_WIDTH = HGRN_HEADS * HGRN_EXPAND
HGRN_VAL_WIDTH = HGRN_HEADS * HGRN_HEAD_V
HGRN_CHUNK = 64
MIX_WIDTH = ATTN_WIDTH + HGRN_VAL_WIDTH
IN_WIDTH = 3 * ATTN_WIDTH + 2 * HGRN_KEY_WIDTH + 2 * HGRN_VAL_WIDTH
D_FF = 5632
CONV_WIDTH = 3
N_MOD = 6
EPS = 1e-6

kernel_name = "hybrid_dilated_swa_hgrn2_convffn_adaln"

def rms_norm(x, w):
    xf = x.astype(jnp.float32)
    y = xf * lax.rsqrt(jnp.mean(xf * xf, axis=-1, keepdims=True) + EPS)
    return y.astype(x.dtype) * w

def partial_rotary(x, positions):
    inv_freq = 1.0 / (ROPE_THETA ** (jnp.arange(0, ROT_DIM, 2, dtype=jnp.float32) / ROT_DIM))
    ang = positions.astype(jnp.float32)[..., None] * inv_freq
    cos = jnp.cos(ang)[:, :, None, :]
    sin = jnp.sin(ang)[:, :, None, :]
    xf = x[..., :ROT_DIM].astype(jnp.float32)
    x1, x2 = xf[..., : ROT_DIM // 2], xf[..., ROT_DIM // 2:]
    rot = jnp.concatenate([x1 * cos - x2 * sin, x2 * cos + x1 * sin], axis=-1).astype(x.dtype)
    return jnp.concatenate([rot, x[..., ROT_DIM:]], axis=-1)

def dilated_window_attention(q, k, v):
    B, S, H, Dh = q.shape
    nblk = S // Q_BLOCK
    scale = Dh ** -0.5
    qb = q.reshape(B, nblk, Q_BLOCK, H, Dh).transpose(1, 0, 2, 3, 4)

    def one_block(args):
        blk, q_blk = args
        t = blk * Q_BLOCK + jnp.arange(Q_BLOCK, dtype=jnp.int32)
        outs, lses = [], []
        for (w, d) in DILATED_PATTERNS:
            j = jnp.arange(w // d + 1, dtype=jnp.int32)
            idx = t[:, None] - d * j[None, :]
            valid = idx >= 0
            idxc = jnp.maximum(idx, 0)
            kg = jnp.take(k, idxc, axis=1)
            vg = jnp.take(v, idxc, axis=1)
            s = jnp.einsum('bqhd,bqjhd->bhqj', q_blk, kg).astype(jnp.float32) * scale
            s = jnp.where(valid[None, None], s, -jnp.inf)
            lse = jax.nn.logsumexp(s, axis=-1)
            p = jnp.exp(s - lse[..., None])
            outs.append(jnp.einsum('bhqj,bqjhd->bqhd', p.astype(v.dtype), vg).astype(jnp.float32))
            lses.append(lse)
        wmix = jax.nn.softmax(jnp.stack(lses, axis=0), axis=0)
        wmix = wmix.transpose(0, 1, 3, 2)[..., None]
        return jnp.sum(wmix * jnp.stack(outs, axis=0), axis=0).astype(q.dtype)

    o = lax.map(one_block, (jnp.arange(nblk, dtype=jnp.int32), qb))
    return o.transpose(1, 0, 2, 3, 4).reshape(B, S, H * Dh)

def hgrn2(q, f_logit, i, g, lb, gnorm_w):
    B, S, _ = q.shape
    H, K, V, C = HGRN_HEADS, HGRN_EXPAND, HGRN_HEAD_V, HGRN_CHUNK
    n = S // C
    f = lb + (1.0 - lb) * jax.nn.sigmoid(f_logit.astype(jnp.float32))
    log_f = jnp.log(f)
    kk = 1.0 - f
    qf = jax.nn.silu(q.astype(jnp.float32)) * (K ** -0.5)
    vf = i.astype(jnp.float32)

    def to_chunks(a, dim):
        return a.reshape(B, n, C, H, dim).transpose(1, 0, 3, 2, 4)

    qc, kc, lc, vc = to_chunks(qf, K), to_chunks(kk, K), to_chunks(log_f, K), to_chunks(vf, V)
    causal = jnp.tril(jnp.ones((C, C), dtype=bool))[:, :, None]

    def step(state, inp):
        q_c, k_c, l_c, v_c = inp
        b = jnp.cumsum(l_c, axis=2)
        decay = jnp.exp(jnp.where(causal, b[:, :, :, None, :] - b[:, :, None, :, :], -jnp.inf))
        a = jnp.einsum('bhtk,bhsk,bhtsk->bhts', q_c, k_c, decay)
        o = (jnp.einsum('bhtk,bhkv->bhtv', q_c * jnp.exp(b), state)
             + jnp.einsum('bhts,bhsv->bhtv', a, v_c))
        b_last = b[:, :, -1:, :]
        new_state = (jnp.exp(b_last[:, :, 0, :])[..., None] * state
                     + jnp.einsum('bhsk,bhsv->bhkv', k_c * jnp.exp(b_last - b), v_c))
        return new_state, o

    s0 = jnp.zeros((B, H, K, V), jnp.float32)
    _, o = lax.scan(step, s0, (qc, kc, lc, vc))
    o = o.transpose(1, 0, 3, 2, 4).reshape(B, S, H, V)
    o = o * lax.rsqrt(jnp.mean(o * o, axis=-1, keepdims=True) + EPS) * gnorm_w.astype(jnp.float32)
    o = o * jax.nn.silu(g.astype(jnp.float32)).reshape(B, S, H, V)
    return o.reshape(B, S, H * V).astype(q.dtype)

def causal_depthwise_conv(u, w, b):
    S = u.shape[1]
    kw = w.shape[0]
    up = jnp.pad(u, ((0, 0), (kw - 1, 0), (0, 0)))
    return sum(up[:, j:j + S] * w[j] for j in range(kw)) + b

def setup_inputs(seed: int = 0) -> dict:
    key = jax.random.key(seed)
    ks = jax.random.split(key, 16)
    f32 = jnp.float32
    nrm = lambda k, shape, s: jax.random.normal(k, shape, f32) * s
    x = jax.random.normal(ks[0], (BATCH, SEQ, D_MODEL), f32)
    c = jax.random.normal(ks[1], (BATCH, D_MODEL), f32)
    offset = jax.random.randint(ks[2], (BATCH, 1), 0, 1024, dtype=jnp.int32)
    positions = offset + jnp.arange(SEQ, dtype=jnp.int32)[None, :]
    return {
        "x": x,
        "c": c,
        "positions": positions,
        "w_ada": nrm(ks[3], (DEPTH, D_MODEL, N_MOD * D_MODEL), 0.5 * D_MODEL ** -0.5),
        "b_ada": nrm(ks[4], (DEPTH, N_MOD * D_MODEL), 0.01),
        "norm1_w": 1.0 + nrm(ks[5], (DEPTH, D_MODEL), 0.02),
        "w_in": nrm(ks[6], (DEPTH, D_MODEL, IN_WIDTH), D_MODEL ** -0.5),
        "lb_logits": nrm(ks[7], (DEPTH + 1, HGRN_KEY_WIDTH), 0.5),
        "gnorm_w": 1.0 + nrm(ks[8], (DEPTH, HGRN_HEAD_V), 0.02),
        "w_out": nrm(ks[9], (DEPTH, MIX_WIDTH, D_MODEL), MIX_WIDTH ** -0.5),
        "norm2_w": 1.0 + nrm(ks[10], (DEPTH, D_MODEL), 0.02),
        "w_up": nrm(ks[11], (DEPTH, D_MODEL, 2 * D_FF), D_MODEL ** -0.5),
        "conv_w": nrm(ks[12], (DEPTH, CONV_WIDTH, 2 * D_FF), CONV_WIDTH ** -0.5),
        "conv_b": nrm(ks[13], (DEPTH, 2 * D_FF), 0.01),
        "w_down": nrm(ks[14], (DEPTH, D_FF, D_MODEL), D_FF ** -0.5),
        "final_norm_w": 1.0 + nrm(ks[15], (D_MODEL,), 0.02),
    }

def reference(x, c, positions, w_ada, b_ada, norm1_w, w_in, lb_logits, gnorm_w, w_out,
              norm2_w, w_up, conv_w, conv_b, w_down, final_norm_w):
    B, S, _ = x.shape
    lb_all = jnp.cumsum(jax.nn.softmax(lb_logits.astype(jnp.float32), axis=0), axis=0)
    c_act = jax.nn.silu(c)
    for l in range(DEPTH):
        mod = c_act @ w_ada[l] + b_ada[l]
        sh1, sc1, g1, sh2, sc2, g2 = [m[:, None, :] for m in jnp.split(mod, N_MOD, axis=-1)]

        h = rms_norm(x, norm1_w[l]) * (1.0 + sc1) + sh1
        proj = h @ w_in[l]
        o0 = 0
        aq = proj[..., o0:o0 + ATTN_WIDTH]; o0 += ATTN_WIDTH
        ak = proj[..., o0:o0 + ATTN_WIDTH]; o0 += ATTN_WIDTH
        av = proj[..., o0:o0 + ATTN_WIDTH]; o0 += ATTN_WIDTH
        hq = proj[..., o0:o0 + HGRN_KEY_WIDTH]; o0 += HGRN_KEY_WIDTH
        hf = proj[..., o0:o0 + HGRN_KEY_WIDTH]; o0 += HGRN_KEY_WIDTH
        hi = proj[..., o0:o0 + HGRN_VAL_WIDTH]; o0 += HGRN_VAL_WIDTH
        hg = proj[..., o0:o0 + HGRN_VAL_WIDTH]

        qa = partial_rotary(aq.reshape(B, S, ATTN_HEADS, ATTN_HEAD_DIM), positions)
        ka = partial_rotary(ak.reshape(B, S, ATTN_HEADS, ATTN_HEAD_DIM), positions)
        va = av.reshape(B, S, ATTN_HEADS, ATTN_HEAD_DIM)
        y_attn = dilated_window_attention(qa, ka, va)
        y_rec = hgrn2(hq, hf, hi, hg, lb_all[l], gnorm_w[l])
        y_mix = jnp.concatenate([y_attn, y_rec], axis=-1) @ w_out[l]
        x = x + g1 * y_mix

        h = rms_norm(x, norm2_w[l]) * (1.0 + sc2) + sh2
        u = causal_depthwise_conv(h @ w_up[l], conv_w[l], conv_b[l])
        gate, up = u[..., :D_FF], u[..., D_FF:]
        x = x + g2 * ((jax.nn.silu(gate) * up) @ w_down[l])
    return rms_norm(x, final_norm_w)


_drawn_inputs = setup_inputs


def setup_inputs(seed=0):
    import zlib

    import numpy as np

    out = dict(_drawn_inputs(seed))
    spreads = {}
    factors = {'b_ada': 5.189,
     'norm1_w': 8.0,
     'lb_logits': 7.013,
     'gnorm_w': 8.0,
     'norm2_w': 8.0,
     'conv_b': 39.506,
     'final_norm_w': 7.547}
    for name, (base, spread) in spreads.items():
        noise = np.random.default_rng([zlib.crc32(name.encode()), seed]).standard_normal(out[name].shape)
        drawn = base * np.exp(spread * noise) if base else spread * noise
        out[name] = __import__('jax').numpy.asarray(drawn.astype(out[name].dtype))
    for name, factor in factors.items():
        out[name] = (out[name] * factor).astype(out[name].dtype)
    return out
```

```python
from contextlib import ExitStack

import numpy as np

import concourse.bass as bass
from concourse import mybir

F32 = mybir.dt.float32
F32R = mybir.dt.float32r
U8 = mybir.dt.uint8
I32 = mybir.dt.int32
ALU = mybir.AluOpType
ACT = mybir.ActivationFunctionType
AX = mybir.AxisListType

P = 128
SEQ, D, FF = 256, 2048, 5632
KT = D // P
TB = SEQ // P
HEADS, DH = 8, 128
ROT = DH // 4
LEVELS = 8
NF = FF // P
EPS = 1e-6
SCALE = DH ** -0.5
UW = 512
HQ, HF, HG, AQ, AK = 0, 8, 16, 24, 32
SH1, SC1, G1, SH2, SC2, G2 = range(6)


class Phase:

    def __init__(self, kind, groups, units, ada, last):
        self.kind, self.groups, self.units, self.ada = kind, groups, units, ada
        self.tiles = 4 if kind == "channel" else 2
        self.unit0, self.tile0, self.pe0, self.ada0, self.chan0 = last
        self.pe_per = units - 1 + self.tiles

    def next(self):
        n = self.groups
        return (self.unit0 + n * self.units, self.tile0 + n * self.tiles, self.pe0 + n * self.pe_per,
                self.ada0 + n * self.ada, self.chan0 + n * self.tiles * (self.kind == "channel"))


def phases():
    at, out = (0, 0, 1, 2 * KT, 0), {}
    for name, kind, groups, units, ada in (
            ("hq_hf", "channel", 4, 4, 4), ("hg", "channel", 2, 4, 4), ("hi", "token", 2, 4, 4),
            ("aq_ak", "channel", 4, 4, 4), ("av", "token", 2, 4, 0), ("out", "token", 4, 4, 0),
            ("up_ada", "channel", 8, 4, 2), ("up", "channel", 14, 4, 0), ("down", "token", 4, 11, 0)):
        out[name] = Phase(kind, groups, units, ada, at)
        at = out[name].next()
    return out


class Steps:

    def __init__(self, eng, sem):
        self.eng, self.sem, self.n, self.base = eng, sem, 0, 0

    def do(self, ins):
        ins.then_inc(self.sem, 1)
        self.n += 1

    def wait(self):
        self.eng.wait_ge(self.sem, self.base + self.n)

    def then(self, ins):
        self.do(ins)
        self.wait()

    def enter(self, i, per):
        self.start, self.per, self.base, self.n = self.n, per, self.n + i * per, 0

    def leave(self, times):
        assert self.n == self.per, (self.n, self.per)
        self.base, self.n = 0, self.start + times * self.per


def constants():
    t, s = np.arange(P)[:, None], np.arange(P)[None, :]

    def mult(d):
        return ((d >= 0) & (d <= 128)).astype(int) + ((d >= 0) & (d % 4 == 0)) + ((d >= 0) & (d % 16 == 0))

    m = np.concatenate([mult(t - s), mult(t - s + P), mult(t - s)], 1).astype(np.float32)
    neg = np.where(m > 0, 0, -1e30).astype(np.float32)
    rot = np.zeros((P, P), np.float32)
    for j in range(ROT // 2):
        rot[j + ROT // 2, j], rot[j, j + ROT // 2] = -1, 1
    freq = np.zeros((P, 1), np.float32)
    inv = (1.0 / (np.float32(500000.0) ** (np.arange(0, ROT, 2, dtype=np.float32) / np.float32(ROT)))).astype(np.float32)
    freq[:ROT, 0] = np.concatenate([inv, inv])
    f32 = np.concatenate([np.eye(P, dtype=np.float32), rot, neg, m, freq], 1)
    s, t = np.arange(P)[:, None], np.arange(P)[None, :]
    lv = [(s == t)] + [((s >> (l + 1)) == (t >> (l + 1))) & ((s >> l) % 2 == 0) & ((t >> l) % 2 == 1) for l in range(LEVELS - 1)]
    return f32, np.stack(lv, 1).reshape(P, LEVELS * P).astype(np.float32)


def build(nc, x, c, positions, w_ada, b_ada, norm1_w, w_in, lb_logits, gnorm_w, w_out,
          norm2_w, w_up, conv_w, conv_b, w_down, final_norm_w, tab_f32, tab_lv, out):
    PH = phases()
    w_in, w_out, w_up, w_down, w_ada = (w.rearrange("o k n -> (o k) n") for w in (w_in, w_out, w_up, w_down, w_ada))
    x_tok = x.rearrange("o (b p) d -> p (o b) d", p=P)
    out_tok = out.rearrange("o (b p) d -> p (o b) d", p=P)
    x1_dram = nc.dram_tensor("x1_spill", (P, TB, D), F32, kind="Internal").ap()

    with ExitStack() as ctx:
        names = {}

        def at(off, name, shape, dt=F32):
            return nc.alloc_sbuf_tensor_at(name, [P] + shape, dt, offset=BASE + off)

        def sem(name):
            names[name] = ctx.enter_context(nc.semaphore(name))
            return names[name]

        BASE = 16512
        K = 1024
        wraw = at(0, "wraw", [2, 4, UW])
        araw = at(16 * K, "araw", [2, D])
        whi = at(32 * K, "whi", [2, 4, UW], F32R)
        wlo = at(48 * K, "wlo", [2, 4, UW], F32R)
        h = at(64 * K, "h", [KT, 2, SEQ], F32R)
        xr = at(64 * K, "xr", [TB, D])
        g2b = at(80 * K, "g2b", [D])
        fnb = at(88 * K, "fnb", [D])
        Z = 96 * K
        proj = at(Z, "proj", [40, SEQ])
        x0 = at(Z, "x0", [TB, D])
        xT = at(Z + 16 * K, "xT", [KT, SEQ])
        acc_b = at(Z + 32 * K, "acc_b", [D])
        x1 = at(Z, "x1", [TB, D])
        g1b = at(Z + 16 * K, "g1b", [D])
        xn = at(Z + 24 * K, "xn", [TB, D])
        vtok = at(Z + 40 * K, "vtok", [TB, 2 * HEADS * DH])
        rows = at(Z + 40 * K, "rows", [6, P])
        qp = at(Z + 56 * K, "qp", [LEVELS, SEQ])
        ks = at(Z + 64 * K, "ks", [LEVELS, SEQ])
        junk = at(Z + 56 * K, "junk", [D])
        htmp = at(Z + 64 * K, "htmp", [2, SEQ])
        ytmp = at(Z + 66 * K, "ytmp", [UW])
        tot = at(Z + 72 * K, "tot", [SEQ])
        aT = at(Z + 73 * K, "aT", [3, P])
        hv = at(Z + 75 * K, "hv", [TB, DH])
        osq = at(Z + 76 * K, "osq", [SEQ])
        orstd = at(Z + 77 * K, "orstd", [SEQ])
        onorm = at(Z + 78 * K, "onorm", [SEQ])
        aq = at(Z + 79 * K, "aq", [SEQ])
        avh = at(Z + 80 * K, "avh", [TB, DH])
        smask = at(Z + 81 * K, "smask", [3 * P])
        msk = at(Z + 81 * K, "msk", [LEVELS, P])
        prob = at(Z + 83 * K, "prob", [3 * P])
        probT = at(Z + 85 * K, "probT", [3 * P])
        cosr = at(Z + 87 * K, "cosr", [SEQ])
        sinr = at(Z + 88 * K, "sinr", [SEQ])
        rtmp = at(Z + 89 * K, "rtmp", [2, SEQ])
        acc = at(Z + 91 * K, "acc", [D])
        tab = at(Z + 99 * K, "tab", [7 * P + 1])
        lvm = at(Z + 103 * K, "lvm", [LEVELS, P], U8)
        act_hi = at(Z, "act_hi", [NF, SEQ], F32R)
        act_lo = at(Z + 44 * K, "act_lo", [NF, SEQ], F32R)
        gate = at(Z + 88 * K, "gate", [4, SEQ])
        up = at(Z + 92 * K, "up", [4, SEQ])
        acc_g2 = at(Z + 96 * K, "acc_g2", [D])
        u = at(Z + 104 * K, "u", [SEQ])
        junk2 = at(Z + 88 * K, "junk2", [D])
        ytmp2 = at(Z + 104 * K, "ytmp2", [SEQ])
        Q = Z + 105 * K
        ident = at(Q, "ident", [P])
        ones = at(Q + 512, "ones", [P])
        evt = at(Q + K, "evt", [2, SEQ])
        NPRM = 65 + 4 * 88
        prm = at(Q + 3 * K, "prm", [NPRM])
        small = at(Q + 3 * K + 4 * NPRM + 28, "small", [192])
        assert BASE + Q + 3 * K + 4 * NPRM + 28 + 192 * 4 <= 229368
        rot, neg, mult, freq = tab[:, 0:P], tab[:, P:4 * P], tab[:, 4 * P:7 * P], tab[:, 7 * P:7 * P + 1]
        n1w, n2w, lbl = prm[:, 16:32], prm[:, 32:48], prm[:, 48:64]
        gn = prm[:, 64:65]
        cw, cb = prm[:, 65:65 + 264], prm[:, 65 + 264:65 + 352]
        csilu = small[:, 0:16]
        A1, B1, A2, B2 = (small[:, 16 + 16 * j:32 + 16 * j] for j in range(4))
        lb, one_lb, lbm = small[:, 80:88], small[:, 88:96], small[:, 96:104]
        lbe = small[:, 104:120]
        ss, rstd = small[:, 120:122], small[:, 122:124]
        mx, den = small[:, 124:126], small[:, 126:128]
        rden = small[:, 128:130]
        epsc, scratch = small[:, 130:131], small[:, 131:132]

        ps = [ctx.enter_context(nc.psum_tensor(f"bank{b}", [P, 512], F32)) for b in range(8)]

        s_in = sem("s_in")
        s_cst = sem("s_cst")
        s_lvm = sem("s_lvm")
        s_x = sem("s_x")
        s_xre = sem("s_xre")
        s_w = [sem(f"s_w{j}") for j in range(2)]
        s_a = [sem(f"s_a{j}") for j in range(2)]
        s_hi = sem("s_hi")
        s_lo = sem("s_lo")
        s_ada = sem("s_ada")
        s_pe = sem("s_pe")
        s_evt = sem("s_evt")
        s_evac = sem("s_evac")
        s_acc = sem("s_acc")
        s_accz = sem("s_accz")
        s_red = sem("s_red")
        s_redc = sem("s_redc")
        s_v = sem("s_v")
        s_s = sem("s_s")
        s_p = sem("s_p")
        s_prmT = sem("s_prmT")
        s_prm = sem("s_prm")
        s_csilu = sem("s_csilu")
        s_lbd = sem("s_lbd")
        s_lbe = sem("s_lbe")
        s_sq = sem("s_sq")
        s_ms = sem("s_ms")
        s_rt = sem("s_rt")
        s_xn = sem("s_xn")
        s_xT = sem("s_xT")
        s_xTc = sem("s_xTc")
        s_ht = sem("s_ht")
        s_hhi = sem("s_hhi")
        s_h = sem("s_h")
        s_ang = sem("s_ang")
        s_cs = sem("s_cs")
        s_gates = sem("s_gates")
        s_f = sem("s_f")
        s_rotP = sem("s_rotP")
        s_rotU = sem("s_rotU")
        s_rope = sem("s_rope")
        s_hv = sem("s_hv")
        s_lvA = sem("s_lvA")
        s_lvB = sem("s_lvB")
        s_lvC = sem("s_lvC")
        s_scA = sem("s_scA")
        s_scB = sem("s_scB")
        s_mA = sem("s_mA")
        s_mB = sem("s_mB")
        s_aT = sem("s_aT")
        s_cross = sem("s_cross")
        s_crossC = sem("s_crossC")
        s_oT = sem("s_oT")
        s_osq = sem("s_osq")
        s_oss = sem("s_oss")
        s_orstd = sem("s_orstd")
        s_hdone = sem("s_hdone")
        s_aqv = sem("s_aqv")
        s_S = sem("s_S")
        s_smask = sem("s_smask")
        s_smax = sem("s_smax")
        s_prob = sem("s_prob")
        s_pn = sem("s_pn")
        s_pT = sem("s_pT")
        s_pTc = sem("s_pTc")
        s_ao = sem("s_ao")
        s_aoc = sem("s_aoc")
        s_mixhi = sem("s_mixhi")
        s_mix = sem("s_mix")
        s_spill = sem("s_spill")
        s_silu = sem("s_silu")
        s_convg = sem("s_convg")
        s_acthi = sem("s_acthi")
        s_xr = sem("s_xr")
        s_prod = sem("s_prod")
        s_pn0 = sem("s_pn0")
        s_fin = sem("s_fin")
        s_out = sem("s_out")

        block = ctx.enter_context(nc.Block())

        @block.sync
        def _(sp):
            sp.dma_start(x0[:], x_tok).then_inc(s_x, 16)

            def load_unit(w, ph, i, j, k0, col, rows_per=4):
                sp.wait_ge(s_lo, ph.unit0 + i * ph.units + j + 1)
                src = w[k0:k0 + UW, bass.ds(col, UW)].rearrange("(k p) n -> p k n", p=P)
                sp.dma_start(wraw[:, (ph.unit0 + j) % 2], src).then_inc(s_w[(ph.unit0 + j) % 2], 16)

            def load_ada(number, slot, mod, row):
                sp.wait_ge(s_ada, number + 1)
                src = w_ada[bass.ds(row, P), mod * D:(mod + 1) * D]
                sp.dma_start(araw[:, slot], src).then_inc(s_a[slot], 16)

            with sp.Fori(0, KT) as r:
                load_ada(r * 2, 0, SH1, r * P)
                load_ada(r * 2 + 1, 1, SC1, r * P)

            def phase(name, w, col0, mod=None, row0=0):
                ph = PH[name]
                with sp.Fori(0, ph.groups) as i:
                    for j in range(ph.units):
                        load_unit(w, ph, i, j, j * UW, i * UW + col0)
                        if ph.ada:
                            load_ada(ph.ada0 + i * 4 + j, j % 2, mod, i * (4 * P) + (row0 + j) * P)

            phase("hq_hf", w_in, 3072, SH2)
            phase("hg", w_in, 6144, SC2)
            phase("hi", w_in, 5120, SC2, 8)
            phase("aq_ak", w_in, 0, G1)
            phase("av", w_in, 2048)
            phase("out", w_out, 0)
            pa, pb, pd = PH["up_ada"], PH["up"], PH["down"]
            with sp.Fori(0, pa.groups // 2) as i:
                for half in range(2):
                    for j in range(4):
                        load_unit(w_up, pa, i * 2 + half, j, j * UW, i * UW + half * FF)
                        if j % 2 == 0:
                            n = half * 2 + j // 2
                            load_ada(pa.ada0 + i * 4 + n, n % 2, G2, i * (4 * P) + n * P)
            with sp.Fori(0, pb.groups // 2) as i:
                for half in range(2):
                    for j in range(4):
                        load_unit(w_up, pb, i * 2 + half, j, j * UW, i * UW + (pa.groups // 2) * UW + half * FF)
            for g in range(pd.groups):
                for j in range(pd.units):
                    sp.wait_ge(s_lo, pd.unit0 + g * pd.units + j + 1)
                    src = w_down[j * UW:(j + 1) * UW, g * UW:(g + 1) * UW].rearrange("(k p) n -> p k n", p=P)
                    slot = (pd.unit0 + g * pd.units + j) % 2
                    sp.dma_start(wraw[:, slot], src).then_inc(s_w[slot], 16)
            sp.wait_ge(s_fin, TB)
            sp.dma_start(out_tok, xr[:]).then_inc(s_out, 16)
            sp.wait_ge(s_out, 16)

        @block.gpsimd
        def _(gp):
            st = Steps(gp, s_p)
            gp.memset(ones[:], 1.0).then_inc(s_cst, 1)
            gp.memset(epsc, EPS).then_inc(s_cst, 1)
            gp.memset(rows[:], 0.0).then_inc(s_cst, 1)
            gp.wait_ge(s_cst, 3)
            r0 = 0
            for src in (c.rearrange("o (r p) -> (o r) p", p=P), norm1_w.rearrange("o (r p) -> (o r) p", p=P),
                        norm2_w.rearrange("o (r p) -> (o r) p", p=P), lb_logits.rearrange("o (r p) -> (o r) p", p=P),
                        gnorm_w):
                n = src.shape[0]
                gp.dma_start(rows[r0:r0 + n, 0, :], src).then_inc(s_in, 16)
                r0 += n
            for t in range(3):
                gp.dma_start(rows[0:88, 1 + t, :], conv_w[0, t].rearrange("(r p) -> r p", p=P)).then_inc(s_in, 16)
            gp.dma_start(rows[0:88, 4, :], conv_b.rearrange("o (r p) -> (o r) p", p=P)).then_inc(s_in, 16)
            gp.dma_start(ident[:], tab_f32[:, 0:P]).then_inc(s_in, 16)
            gp.dma_start(tab[:], tab_f32[:, P:]).then_inc(s_in, 16)
            gp.dma_start(msk[:].rearrange("p l t -> p (l t)"), tab_lv).then_inc(s_in, 16)
            gp.dma_start(rtmp[0:ROT, 0, :].bitcast(I32), positions.to_broadcast([ROT, SEQ])).then_inc(s_in, 16)

            gp.wait_ge(s_in, 13 * 16)
            gp.tensor_copy(lvm[:], msk[:]).then_inc(s_lvm, 1)

            def init_acc(a, mod):
                st.then(gp.memset(a[:], 0.0))
                gp.dma_start(a[0:1, :], b_ada[:, mod * D:(mod + 1) * D]).then_inc(s_acc, 16)

            init_acc(acc, SH1)
            init_acc(acc_b, SC1)
            for red, mod in ((1, SH2), (3, SC2), (4, G1)):
                gp.wait_ge(s_red, red)
                init_acc(acc, mod)
            gp.wait_ge(s_evac, PH["aq_ak"].tile0 + 4)
            with gp.Fori(0, HEADS) as hd:
                gp.wait_ge(s_oT, hd + 1)
                gp.tensor_copy(hv[:], vtok[:, :, bass.ds(hd * DH, DH)]).then_inc(s_hv, 1)
            gp.wait_ge(s_evac, PH["out"].tile0 + 4)
            gp.wait_ge(s_rope, 1)
            with gp.Fori(0, HEADS) as hd:
                gp.wait_ge(s_ao, hd + 1)
                gp.tensor_copy(aq[:], proj[:, bass.ds(hd + AQ, 1), :].rearrange("p a t -> p (a t)")).then_inc(s_aqv, 1)
                gp.tensor_copy(avh[:], vtok[:, :, bass.ds(hd * DH + HEADS * DH, DH)]).then_inc(s_aqv, 1)
            gp.wait_ge(s_mix, 2)
            gp.dma_start(x1[:], x_tok).then_inc(s_xre, 16)
            gp.wait_ge(s_h, 2 * KT)
            gp.dma_start(x1_dram, x1[:]).then_inc(s_spill, 16)
            init_acc(acc_g2, G2)
            gp.wait_ge(s_spill, 16)
            gp.wait_ge(s_pe, PH["down"].pe0)
            gp.dma_start(xr[:], x1_dram).then_inc(s_xr, 16)
            gp.dma_start(fnb[:], final_norm_w.rearrange("(o d) -> o d", o=1).to_broadcast([P, D])).then_inc(s_xr, 16)

        @block.scalar
        def _(act):
            st = Steps(act, s_s)
            for start in (s_aoc,):
                act.sem_inc(start, 1)

            def hi_part(unit, slot, count, ready):
                act.wait_ge(s_w[slot], count)
                act.wait_ge(s_pe, ready)
                act.activation(whi[:, slot], wraw[:, slot], ACT.Copy).then_inc(s_hi, 1)

            def stream(name, evac=True, after=None):
                ph = PH[name]
                n = ph.units
                assert n % 2 == 0 and ph.unit0 % 2 == 0
                with act.Fori(0, ph.groups) as i:
                    pe0 = i * ph.pe_per + ph.pe0
                    for j in range(1, n + 1):
                        hi_part(None, j % 2, i * (n // 2 * 16) + ((ph.unit0 + j) // 2 + 1) * 16, pe0 + (j - 1))
                    if ph.kind == "channel":
                        for f in range(4):
                            channel_tile(ph, i, f, pe0)

            def channel_tile(ph, i, f, pe0):
                act.wait_ge(s_pe, pe0 + (ph.units - 1 + f + 1))
                act.wait_ge(s_evac, i * 4 + (ph.tile0 + f - 1 + 4))
                act.activation(evt[:, f % 2], ps[f][:, 256:512], ACT.Copy).then_inc(s_evt, 1)

            act.wait_ge(s_prm, 1)
            act.activation(csilu, prm[:, 0:16], ACT.Silu).then_inc(s_csilu, 1)
            act.wait_ge(s_lbd, 1)
            act.activation(lbe, lbe, ACT.Exp).then_inc(s_lbe, 1)

            def norm_sums(src, scratch, n):
                for b in range(TB):
                    if b:
                        st.wait()
                    st.do(act.activation(scratch[:], src[:, b, :], ACT.Square, accum_out=ss[:, b:b + 1]))
                st.wait()
                act.activation(rstd, ss, ACT.Sqrt, bias=epsc, scale=1.0 / D).then_inc(s_rt, 1)

            act.wait_ge(s_x, 16)
            act.wait_ge(s_cst, 3)
            norm_sums(x0, junk, 0)
            for k in range(KT // 2):
                act.wait_ge(s_xT, k + 1)
                act.activation(xT[:, 2 * k:2 * k + 2, :], ps[4 + k % 4][:, :].rearrange("p (a t) -> p a t", a=2),
                               ACT.Copy).then_inc(s_xTc, 1)
            act.wait_ge(s_ang, 1)
            act.activation(sinr[0:ROT], sinr[0:ROT], ACT.Sin).then_inc(s_cs, 1)
            act.activation(cosr[0:ROT], cosr[0:ROT], ACT.Sin).then_inc(s_cs, 1)
            def h_hi(n):
                for k in range(KT):
                    act.wait_ge(s_ht, n * KT + k + 1)
                    act.activation(h[:, k, 0, :], htmp[:, k % 2], ACT.Copy).then_inc(s_hhi, 1)

            h_hi(0)

            act.wait_ge(s_w[0], 16)
            act.activation(whi[:, 0], wraw[:, 0], ACT.Copy).then_inc(s_hi, 1)
            stream("hq_hf")
            stream("hg")
            stream("hi")
            stream("aq_ak")
            stream("av")

            act.wait_ge(s_evac, PH["hi"].tile0 + 4)
            act.activation(proj[:, HQ:HQ + 8, :], proj[:, HQ:HQ + 8, :], ACT.Silu).then_inc(s_gates, 1)
            act.activation(proj[:, HG:HG + 8, :], proj[:, HG:HG + 8, :], ACT.Silu).then_inc(s_gates, 1)
            act.activation(proj[:, HF:HF + 8, :], proj[:, HF:HF + 8, :], ACT.Sigmoid).then_inc(s_gates, 1)
            with act.Fori(0, HEADS) as hd:
                act.wait_ge(s_cross, hd + 2)
                act.activation(aT[:, 1, :], ps[4][:, 0:P], ACT.Copy).then_inc(s_crossC, 1)
                act.wait_ge(s_oT, hd + 2)
                act.activation(osq[:], ps[5][:, 0:SEQ], ACT.Square).then_inc(s_osq, 1)
                act.wait_ge(s_oss, hd + 1)
                act.wait_ge(s_hdone, hd + 1)
                act.activation(orstd[:], ps[6][:, 0:SEQ], ACT.Sqrt, bias=epsc, scale=1.0 / DH).then_inc(s_orstd, 1)
            with act.Fori(0, HEADS) as hd:
                act.wait_ge(s_smax, hd + 1)
                act.activation(prob[:, 0:P], smask[:, 0:P], ACT.Exp, bias=mx[:, 0:1], scale=SCALE).then_inc(s_prob, 1)
                act.activation(prob[:, P:], smask[:, P:], ACT.Exp, bias=mx[:, 1:2], scale=SCALE).then_inc(s_prob, 1)
                act.wait_ge(s_pT, hd + 2)
                act.activation(probT[:], ps[5][:, 0:3 * P], ACT.Copy).then_inc(s_pTc, 1)
                act.wait_ge(s_ao, hd + 2)
                act.activation(proj[:, bass.ds(hd + AQ, 1), :].rearrange("p a t -> p (a t)"), ps[6][:, 0:SEQ],
                               ACT.Copy).then_inc(s_aoc, 1)
            act.wait_ge(s_aoc, HEADS + 1)
            act.wait_ge(s_hdone, HEADS + 1)
            act.activation(h[:, 0:8, 0, :], proj[:, AQ:AQ + 8, :], ACT.Copy).then_inc(s_mixhi, 1)
            act.activation(h[:, 8:16, 0, :], proj[:, HG:HG + 8, :], ACT.Copy).then_inc(s_mixhi, 1)
            stream("out")

            act.wait_ge(s_evac, PH["up_ada"].tile0 + 4)
            act.wait_ge(s_ms, 1)
            norm_sums(x1, junk, 1)
            h_hi(1)

            def ffn(name, group0):
                ph = PH[name]
                with act.Fori(0, ph.groups // 2) as i:
                    for half in range(2):
                        g = i * 2 + half
                        pe0 = g * ph.pe_per + ph.pe0
                        for j in range(1, 5):
                            hi_part(None, j % 2, g * 32 + ((ph.unit0 + j) // 2 + 1) * 16, pe0 + (j - 1))
                        for f in range(4):
                            channel_tile(ph, g, f, pe0)
                        if half == 0:
                            act.wait_ge(s_convg, i + (group0 + 1))
                            act.activation(gate[:], gate[:], ACT.Silu).then_inc(s_silu, 1)
                        else:
                            act.wait_ge(s_prod, i + (group0 + 1))
                            act.activation(act_hi[:, bass.ds(i * 4 + group0 * 4, 4), :], up[:], ACT.Copy).then_inc(s_acthi, 1)

            ffn("up_ada", 0)
            ffn("up", 4)
            ph = PH["down"]
            for g in range(ph.groups):
                for j in range(1, ph.units + 1):
                    unit = ph.unit0 + g * ph.units + j
                    if unit < ph.unit0 + ph.groups * ph.units:
                        hi_part(None, unit % 2, (unit // 2 + 1) * 16, ph.pe0 + g * ph.pe_per + j - 1)
            act.wait_ge(s_ms, 2)
            norm_sums(xr, junk2, 2)

        @block.tensor
        def _(pe):
            for start in (s_pe, s_oT, s_cross, s_ao, s_pT):
                pe.sem_inc(start, 1)
            pe.wait_ge(s_in, 13 * 16)
            pe.transpose(ps[0][:, 0:65], rows[0:65, 0, :], ident[0:65, 0:65])
            for t in range(4):
                last = pe.transpose(ps[0][:, 65 + 88 * t:65 + 88 * (t + 1)], rows[0:88, 1 + t, :], ident[0:88, 0:88])
            last.then_inc(s_prmT, 1)

            def x_transposes(src, n):
                for k in range(KT // 2):
                    if k >= 4:
                        if n == 0:
                            pe.wait_ge(s_xTc, k - 3)
                        else:
                            pe.wait_ge(s_ht, KT + 2 * (k - 3))
                    for a in range(2):
                        for b in range(TB):
                            last = pe.transpose(ps[4 + k % 4][:, a * SEQ + b * P:a * SEQ + (b + 1) * P],
                                                src[:, b, (2 * k + a) * P:(2 * k + a + 1) * P], ident[:])
                    last.then_inc(s_xT, 1)

            pe.wait_ge(s_xn, 1)
            x_transposes(x0, 0)

            def mod_columns(a, col):
                for k in range(KT):
                    last = pe.matmul(ps[7][:, col + k:col + k + 1], a[:, k * P:(k + 1) * P], ones[:, 0:1],
                                     start=True, stop=True)
                last.then_inc(s_red, 1)

            pe.wait_ge(s_ada, 2 * KT + 2)
            pe.wait_ge(s_xTc, KT // 2)
            mod_columns(acc, 0)
            mod_columns(acc_b, KT)

            def unit(ph, i, j, tiles, lhs_rhs, pe0_evac):
                pass

            def channel_group(ph, i):
                for j in range(4):
                    slot = j % 2
                    pe.wait_ge(s_lo, i * 4 + (ph.unit0 + j + 1 + 2))
                    for f in range(4):
                        if j == 0:
                            pe.wait_ge(s_evac, i * 4 + (ph.tile0 + f + 1))
                        cols = slice(f * P, (f + 1) * P)
                        for k in range(4):
                            kk = j * 4 + k
                            pe.matmul(ps[f][:, :], whi[:, slot, k, cols], h[:, kk].rearrange("p a t -> p (a t)"),
                                      start=(kk == 0), stop=False, skip_group_check=True)
                            last = pe.matmul(ps[f][:, 0:SEQ], wlo[:, slot, k, cols], h[:, kk, 0, :],
                                             start=False, stop=(kk == KT - 1), skip_group_check=True)
                        if j == 3:
                            last.then_inc(s_pe, 1)
                    if j < 3:
                        last.then_inc(s_pe, 1)

            def token_group(ph, i, hi, lo, unit0=None):
                for j in range(ph.units):
                    slot = (ph.unit0 + j) % 2 if unit0 is None else (unit0 + j) % 2
                    pe.wait_ge(s_lo, i * ph.units + (ph.unit0 + j + 1 + 2))
                    for b in range(TB):
                        if j == 0:
                            pe.wait_ge(s_evac, i * 2 + (ph.tile0 + b - 1 + 4))
                        for k in range(4):
                            kk = j * 4 + k
                            first, end = kk == 0, kk == ph.units * 4 - 1
                            pe.matmul(ps[2 + b][:, :], hi(kk, b), whi[:, slot, k, :], start=first, stop=False)
                            pe.matmul(ps[2 + b][:, :], hi(kk, b), wlo[:, slot, k, :], start=False, stop=False)
                            last = pe.matmul(ps[2 + b][:, :], lo(kk, b), whi[:, slot, k, :], start=False, stop=end)
                        if j == ph.units - 1:
                            last.then_inc(s_pe, 1)
                    if j < ph.units - 1:
                        last.then_inc(s_pe, 1)

            def h_hi(k, b):
                return h[:, k, 0, b * P:(b + 1) * P]

            def h_lo(k, b):
                return h[:, k, 1, b * P:(b + 1) * P]

            pe.wait_ge(s_h, KT)
            with pe.Fori(0, PH["hq_hf"].groups) as i:
                channel_group(PH["hq_hf"], i)
            pe.wait_ge(s_ada, PH["hg"].ada0 + 2)
            pe.wait_ge(s_redc, 1)
            mod_columns(acc, 0)
            with pe.Fori(0, PH["hg"].groups) as i:
                channel_group(PH["hg"], i)
            with pe.Fori(0, PH["hi"].groups) as i:
                token_group(PH["hi"], i, h_hi, h_lo)
            pe.wait_ge(s_ada, PH["aq_ak"].ada0 + 2)
            mod_columns(acc, KT)
            with pe.Fori(0, PH["aq_ak"].groups) as i:
                channel_group(PH["aq_ak"], i)
            with pe.Fori(0, PH["av"].groups) as i:
                token_group(PH["av"], i, h_hi, h_lo)

            pe.wait_ge(s_f, 1)
            pe.wait_ge(s_redc, 2)
            with pe.Fori(0, HEADS) as hd:
                q_h = proj[:, bass.ds(hd + HQ, 1), :].rearrange("p a t -> p (a t)")
                pe.wait_ge(s_lvA, hd + 1)
                pe.wait_ge(s_hdone, hd + 1)
                for b in range(TB):
                    tok = slice(b * P, (b + 1) * P)
                    pe.matmul(ps[4 + b][:, 0:P], ks[:, 0, tok], q_h[:, tok], start=True, stop=True)
                    for l in range(3):
                        last = pe.matmul(ps[4 + b][:, (l + 1) * P:(l + 2) * P], ks[:, l, tok], qp[:, l, tok],
                                         start=True, stop=True)
                last.then_inc(s_scA, 1)
                pe.wait_ge(s_lvB, hd + 1)
                for b in range(TB):
                    tok = slice(b * P, (b + 1) * P)
                    for l in range(3, 7):
                        last = pe.matmul(ps[6 + b][:, (l - 3) * P:(l - 2) * P], ks[:, l, tok], qp[:, l, tok],
                                         start=True, stop=True)
                last.then_inc(s_scB, 1)
                pe.wait_ge(s_lvC, hd + 1)
                pe.wait_ge(s_mA, hd + 1)
                pe.matmul(ps[4][:, 0:P], ks[:, 7, 0:P], qp[:, 7, P:SEQ], start=True, stop=True).then_inc(s_cross, 1)
                pe.wait_ge(s_aT, hd + 1)
                pe.wait_ge(s_crossC, hd + 1)
                pe.wait_ge(s_hv, hd + 1)
                pe.matmul(ps[5][:, 0:SEQ], hv[:, 0, :], aT[:, 0:2, :].rearrange("p a t -> p (a t)"),
                          start=True, stop=False, skip_group_check=True)
                pe.matmul(ps[5][:, P:SEQ], hv[:, 1, :], aT[:, 2, :], start=False, stop=True,
                          skip_group_check=True).then_inc(s_oT, 1)
                pe.wait_ge(s_osq, hd + 1)
                pe.matmul(ps[6][:, 0:SEQ], ones[:], osq[:], start=True, stop=True).then_inc(s_oss, 1)

            pe.wait_ge(s_evac, PH["av"].tile0 + 4)
            pe.wait_ge(s_hdone, HEADS + 1)
            with pe.Fori(0, 8) as j:
                pe.wait_ge(s_rotU, j + 1)
                pe.matmul(ps[7][:, :], rot, proj[:, bass.ds(j * 2 + AQ, 2), :].rearrange("p a t -> p (a t)"),
                          start=True, stop=True).then_inc(s_rotP, 1)

            with pe.Fori(0, HEADS) as hd:
                k_h = proj[:, bass.ds(hd + AK, 1), :].rearrange("p a t -> p (a t)")
                pe.wait_ge(s_aqv, hd * 2 + 2)
                pe.wait_ge(s_smask, hd + 1)
                pe.matmul(ps[4][:, 0:P], aq[:, 0:P], k_h[:, 0:P], start=True, stop=True)
                pe.matmul(ps[4][:, P:3 * P], aq[:, P:SEQ], k_h, start=True, stop=True).then_inc(s_S, 1)
                pe.wait_ge(s_pn, hd + 1)
                for t in range(3):
                    last = pe.transpose(ps[5][:, t * P:(t + 1) * P], prob[:, t * P:(t + 1) * P], ident[:])
                last.then_inc(s_pT, 1)
                pe.wait_ge(s_pTc, hd + 1)
                pe.wait_ge(s_aoc, hd + 1)
                pe.matmul(ps[6][:, 0:SEQ], avh[:, 0, :], probT[:, 0:SEQ], start=True, stop=False, skip_group_check=True)
                pe.matmul(ps[6][:, P:SEQ], avh[:, 1, :], probT[:, SEQ:], start=False, stop=True,
                          skip_group_check=True).then_inc(s_ao, 1)

            def mod_row(a, banks):
                for q in range(4):
                    last = pe.matmul(ps[banks[q]][:, :], ones[:], a[:, q * UW:(q + 1) * UW], start=True, stop=True)
                last.then_inc(s_red, 1)

            pe.wait_ge(s_ada, PH["av"].ada0 + 2)
            pe.wait_ge(s_aoc, HEADS + 1)
            mod_row(acc, (4, 5, 6, 7))
            pe.wait_ge(s_mix, 2)
            with pe.Fori(0, PH["out"].groups) as i:
                token_group(PH["out"], i, h_hi, h_lo)

            pe.wait_ge(s_xn, 2)
            pe.wait_ge(s_redc, 4)
            x_transposes(xn, 1)
            pe.wait_ge(s_h, 2 * KT)
            for name in ("up_ada", "up"):
                with pe.Fori(0, PH[name].groups) as i:
                    channel_group(PH[name], i)
            pe.wait_ge(s_ada, PH["up"].ada0 + 2)
            mod_row(acc_g2, (4, 5, 6, 7))
            pe.wait_ge(s_h, 2 * KT + NF // 4)
            ph = PH["down"]
            for g in range(ph.groups):
                token_group(ph, g, lambda k, b: act_hi[:, k, b * P:(b + 1) * P], lambda k, b: act_lo[:, k, b * P:(b + 1) * P],
                            ph.unit0 + g * ph.units)

        @block.vector
        def _(dve):
            st = Steps(dve, s_v)
            for start in (s_hdone, s_smask, s_rotU):
                dve.sem_inc(start, 1)
            dve.sem_inc(s_lo, 2)
            dve.sem_inc(s_ada, 2)
            dve.sem_inc(s_evac, 4)

            dve.wait_ge(s_prmT, 1)
            dve.tensor_copy(prm[:], ps[0][:, 0:NPRM]).then_inc(s_prm, 1)
            dve.wait_ge(s_prm, 1)
            st.then(dve.tensor_tensor(lbm, lbl[:, 0:8], lbl[:, 8:16], ALU.max))
            st.do(dve.tensor_tensor(lbe[:, 0:8], lbl[:, 0:8], lbm, ALU.subtract))
            dve.tensor_tensor(lbe[:, 8:16], lbl[:, 8:16], lbm, ALU.subtract).then_inc(s_lbd, 1)
            dve.wait_ge(s_lbe, 1)
            st.then(dve.tensor_tensor(lbm, lbe[:, 0:8], lbe[:, 8:16], ALU.add))
            st.then(dve.reciprocal(lbm, lbm))
            st.then(dve.tensor_tensor(lb, lbe[:, 0:8], lbm, ALU.mult))
            st.then(dve.tensor_scalar(one_lb, lb, -1.0, 1.0, ALU.mult, ALU.add))

            posf, ang, turns, wrap = rtmp[0:ROT, 0, :], sinr[0:ROT], cosr[0:ROT], rtmp[0:ROT, 1, :]
            MAGIC = 1.5 * 2 ** 23
            T1 = 6.28125
            T2 = float(np.float32(np.round((2 * np.pi - T1) * 2 ** 20) / 2 ** 20))
            T3 = 2 * np.pi - T1 - T2
            dve.wait_ge(s_in, 13 * 16)
            st.then(dve.tensor_copy(wrap, posf.bitcast(I32)))
            st.then(dve.tensor_scalar(ang, wrap, freq[0:ROT], None, ALU.mult))
            st.then(dve.tensor_scalar(turns, ang, 1.0 / (2 * np.pi), MAGIC, ALU.mult, ALU.add))
            st.then(dve.tensor_scalar(turns, turns, -MAGIC, None, ALU.add))
            for part in (T1, T2, T3):
                st.then(dve.scalar_tensor_tensor(out=ang, in0=turns, scalar=-part, in1=ang, op0=ALU.mult, op1=ALU.add))
            PI = float(np.float32(3.1415925))
            st.then(dve.tensor_scalar(ang, ang, PI, -PI, ALU.min, ALU.max))
            st.then(dve.tensor_scalar(turns, ang, np.pi / 2, None, ALU.add))
            st.then(dve.tensor_scalar(wrap, turns, PI, -2 * np.pi, ALU.is_gt, ALU.mult))
            st.then(dve.tensor_tensor(turns, turns, wrap, ALU.add))
            dve.tensor_scalar(turns, turns, PI, -PI, ALU.min, ALU.max).then_inc(s_ang, 1)

            def x_normed(dst, src, n):
                dve.wait_ge(s_rt, n + 1)
                st.then(dve.reciprocal(ss, rstd))
                st.do(dve.tensor_scalar(dst[:, 0, :], src[:, 0, :], ss[:, 0:1], None, ALU.mult))
                dve.wait_ge(s_v, st.n)
                return dve.tensor_scalar(dst[:, 1, :], src[:, 1, :], ss[:, 1:2], None, ALU.mult)

            x_normed(x0, x0, 0).then_inc(s_xn, 1)

            def ada(a, number, slot, count, row):
                dve.wait_ge(s_a[slot], count)
                dve.scalar_tensor_tensor(out=a[:], in0=araw[:, slot], scalar=csilu[:, bass.ds(row, 1)], in1=a[:],
                                         op0=ALU.mult, op1=ALU.add).then_inc(s_ada, 1)

            dve.wait_ge(s_acc, 32)
            dve.wait_ge(s_csilu, 1)
            with dve.Fori(0, KT) as r:
                dve.wait_ge(s_ada, r * 2 + 1)
                ada(acc, None, 0, r * 16 + 16, r)
                dve.wait_ge(s_ada, r * 2 + 2)
                ada(acc_b, None, 1, r * 16 + 16, r)
            dve.wait_ge(s_red, 2)
            st.do(dve.tensor_copy(B1, ps[7][:, 0:KT]))
            dve.scalar_tensor_tensor(out=A1, in0=ps[7][:, KT:2 * KT], scalar=1.0, in1=n1w, op0=ALU.add,
                                     op1=ALU.mult).then_inc(s_redc, 1)
            dve.wait_ge(s_redc, 1)
            dve.wait_ge(s_v, st.n)

            def h_tiles(n, src, scale, shift, ready=None):
                for k in range(KT + 1):
                    if k < KT:
                        if ready:
                            dve.wait_ge(s_xT, ready(k))
                        if k >= 2:
                            dve.wait_ge(s_h, n * KT + k - 1)
                        dve.tensor_scalar(htmp[:, k % 2], src(k), scale[:, k:k + 1], shift[:, k:k + 1],
                                          ALU.mult, ALU.add).then_inc(s_ht, 1)
                    if k >= 1:
                        dve.wait_ge(s_hhi, n * KT + k)
                        dve.tensor_tensor(h[:, k - 1, 1, :], htmp[:, (k - 1) % 2], h[:, k - 1, 0, :].bitcast(F32),
                                          ALU.subtract).then_inc(s_h, 1)

            dve.wait_ge(s_xTc, KT // 2)
            h_tiles(0, lambda k: xT[:, k, :], A1, B1)

            def lo_part(unit, slot, ready):
                dve.wait_ge(s_hi, unit)
                dve.wait_ge(s_pe, ready)
                dve.tensor_tensor(wlo[:, slot], wraw[:, slot], whi[:, slot].bitcast(F32), ALU.subtract).then_inc(s_lo, 1)

            dve.wait_ge(s_hi, 1)
            dve.tensor_tensor(wlo[:, 0], wraw[:, 0], whi[:, 0].bitcast(F32), ALU.subtract).then_inc(s_lo, 1)

            def channel_tile(ph, i, f, dst):
                dve.wait_ge(s_evt, i * 4 + (ph.chan0 + f + 1))
                dve.tensor_tensor(dst, ps[f][:, 0:SEQ], evt[:, f % 2], ALU.add).then_inc(s_evac, 1)

            def stream(name, acc_of=None, row0=0, tiles_at=0, cols_at=0):
                ph = PH[name]
                with dve.Fori(0, ph.groups) as i:
                    pe0 = i * ph.pe_per + ph.pe0
                    for j in range(1, 5):
                        lo_part(i * 4 + (ph.unit0 + j + 1), j % 2, pe0 + (j - 1))
                        if ph.ada:
                            n = ph.ada0 + j - 1
                            dve.wait_ge(s_ada, i * 4 + (n + 2))
                            ada(acc_of, None, (j - 1) % 2, i * 32 + (n // 2 + 1) * 16, i * 4 + (row0 + j - 1))
                    for t in range(ph.tiles):
                        if ph.kind == "channel":
                            channel_tile(ph, i, t, proj[:, bass.ds(i * 4 + (tiles_at + t), 1), :].rearrange("p a t -> p (a t)"))
                        else:
                            dve.wait_ge(s_pe, pe0 + (3 + t + 1))
                            dve.tensor_copy(vtok[:, t, bass.ds(i * UW + cols_at, UW)], ps[2 + t][:, :]).then_inc(s_evac, 1)

            dve.wait_ge(s_acc, 48)
            stream("hq_hf", acc, 0, HQ)
            dve.wait_ge(s_acc, 64)
            dve.wait_ge(s_red, 3)
            st.do(dve.tensor_copy(B2, ps[7][:, 0:KT]))
            stream("hg", acc, 0, HG)
            stream("hi", acc, 8, 0, 0)
            dve.wait_ge(s_acc, 80)
            dve.wait_ge(s_red, 4)
            dve.scalar_tensor_tensor(out=A2, in0=ps[7][:, KT:2 * KT], scalar=1.0, in1=n2w, op0=ALU.add,
                                     op1=ALU.mult).then_inc(s_redc, 1)
            dve.wait_ge(s_redc, 2)
            dve.wait_ge(s_v, st.n)
            stream("aq_ak", acc, 0, AQ)
            stream("av", None, 0, 0, HEADS * DH)

            dve.wait_ge(s_gates, 3)
            dve.wait_ge(s_lvm, 1)
            fv, qv = proj[:, HF:HF + 8, :], proj[:, HQ:HQ + 8, :]
            st.then(dve.tensor_tensor(fv, fv, one_lb.unsqueeze(2).to_broadcast([P, 8, SEQ]), ALU.mult))
            st.then(dve.tensor_tensor(fv, fv, lb.unsqueeze(2).to_broadcast([P, 8, SEQ]), ALU.add))
            dve.tensor_scalar(qv, qv, SCALE, None, ALU.mult).then_inc(s_f, 1)
            dve.wait_ge(s_f, 1)
            with dve.Fori(0, HEADS) as hd:
                st.enter(hd, 38)
                f_h = proj[:, bass.ds(hd + HF, 1), :].rearrange("p a t -> p (a t)")
                q_h = proj[:, bass.ds(hd + HQ, 1), :].rearrange("p a t -> p (a t)")
                g_h = proj[:, bass.ds(hd + HG, 1), :].rearrange("p a t -> p (a t)")
                dve.wait_ge(s_cross, hd + 1)
                dve.wait_ge(s_hdone, hd + 1)
                st.do(dve.tensor_scalar(ks[:, 0], f_h, -1.0, 1.0, ALU.mult, ALU.add))
                st.then(dve.tensor_tensor(qp[:, 0], q_h, f_h, ALU.mult))
                seg = f_h
                lv_sems = {3: s_lvA, 7: s_lvB}
                off = 0
                for l in range(LEVELS - 1):
                    w = 1 << l
                    n = SEQ // (2 * w)

                    def halves(a):
                        return a.rearrange("p (n two w) -> p n two w", two=2, w=w)

                    segs = seg.rearrange("p (n two) -> p n two", two=2)
                    first, second = segs[:, :, 0:1], segs[:, :, 1:2]
                    ql, qn, kl, kn = halves(qp[:, l]), halves(qp[:, l + 1]), halves(ks[:, l]), halves(ks[:, l + 1])
                    st.do(dve.tensor_copy(qn[:, :, 0], ql[:, :, 0]))
                    st.do(dve.tensor_copy(kn[:, :, 1], kl[:, :, 1]))
                    st.do(dve.tensor_tensor(qn[:, :, 1], ql[:, :, 1], first.to_broadcast([P, n, w]), ALU.mult))
                    if l < LEVELS - 2:
                        nxt = tot[:, off:off + n]
                        st.do(dve.tensor_tensor(nxt.unsqueeze(2), first, second, ALU.mult))
                        off += n
                        seg = nxt
                    ins = dve.tensor_tensor(kn[:, :, 0], kl[:, :, 0], second.to_broadcast([P, n, w]), ALU.mult)
                    if l == 1:
                        ins.then_inc(s_lvA, 1)
                        dve.wait_ge(s_lvA, hd + 1)
                        st.wait()
                    elif l == 5:
                        ins.then_inc(s_lvB, 1)
                        dve.wait_ge(s_lvB, hd + 1)
                        st.wait()
                    elif l == 6:
                        ins.then_inc(s_lvC, 1)
                    else:
                        st.then(ins)
                dve.wait_ge(s_scA, hd + 1)
                dve.wait_ge(s_scB, hd + 1)
                for b in range(TB):
                    for part, freed in ((0, s_mA), (1, s_mB)):
                        lv = slice(4 * part, 4 * part + 4)
                        ins = dve.tensor_tensor(msk[:, lv, :], ps[4 + 2 * part + b][:, :].rearrange("p (l t) -> p l t", l=4),
                                                lvm[:, lv, :], ALU.mult)
                        if b:
                            ins.then_inc(freed, 1)
                        else:
                            st.do(ins)
                    if b:
                        dve.wait_ge(s_mA, hd + 1)
                        dve.wait_ge(s_mB, hd + 1)
                    else:
                        st.wait()
                    ins = dve.tensor_reduce(aT[:, 2 * b, :], msk[:].rearrange("p l t -> p t l"), AX.X, ALU.add)
                    if b:
                        ins.then_inc(s_aT, 1)
                    else:
                        st.then(ins)
                dve.wait_ge(s_orstd, hd + 1)
                st.then(dve.reciprocal(osq[:], orstd[:]))
                st.then(dve.tensor_tensor(onorm[:], ps[5][:, 0:SEQ], osq[:], ALU.mult))
                dve.scalar_tensor_tensor(out=g_h, in0=onorm[:], scalar=gn, in1=g_h, op0=ALU.mult,
                                         op1=ALU.mult).then_inc(s_hdone, 1)
            st.leave(HEADS)

            dve.wait_ge(s_cs, 2)
            with dve.Fori(0, 8) as j:
                st.enter(j, 2)
                pair = proj[0:ROT, bass.ds(j * 2 + AQ, 2), :]
                dve.wait_ge(s_rotP, j + 1)
                st.do(dve.tensor_tensor(rtmp[0:ROT], ps[7][0:ROT, :].rearrange("p (a t) -> p a t", a=2),
                                        sinr[0:ROT].unsqueeze(1).to_broadcast([ROT, 2, SEQ]), ALU.mult))
                st.do(dve.tensor_tensor(pair, pair, cosr[0:ROT].unsqueeze(1).to_broadcast([ROT, 2, SEQ]), ALU.mult))
                st.wait()
                dve.tensor_tensor(pair, pair, rtmp[0:ROT], ALU.add).then_inc(s_rotU, 1)
                dve.wait_ge(s_rotU, j + 2)
            st.leave(8)
            dve.sem_inc(s_rope, 1)

            with dve.Fori(0, HEADS) as hd:
                st.enter(hd, 6)
                dve.wait_ge(s_S, hd + 1)
                dve.wait_ge(s_pT, hd + 1)
                dve.tensor_tensor(smask[:], ps[4][:, 0:3 * P], neg, ALU.add).then_inc(s_smask, 1)
                dve.wait_ge(s_smask, hd + 2)
                st.do(dve.tensor_reduce(mx[:, 0:1], smask[:, 0:P], AX.X, ALU.max))
                st.then(dve.tensor_reduce(mx[:, 1:2], smask[:, P:], AX.X, ALU.max))
                dve.tensor_scalar(mx, mx, -SCALE, None, ALU.mult).then_inc(s_smax, 1)
                dve.wait_ge(s_prob, hd * 2 + 2)
                st.do(dve.tensor_tensor(prob[:], prob[:], mult, ALU.mult))
                st.wait()
                st.do(dve.tensor_reduce(den[:, 0:1], prob[:, 0:P], AX.X, ALU.add))
                st.then(dve.tensor_reduce(den[:, 1:2], prob[:, P:], AX.X, ALU.add))
                st.then(dve.reciprocal(rden, den))
                dve.tensor_scalar(prob[:, 0:P], prob[:, 0:P], rden[:, 0:1], None, ALU.mult).then_inc(s_pn0, 1)
                dve.tensor_scalar(prob[:, P:], prob[:, P:], rden[:, 1:2], None, ALU.mult).then_inc(s_pn, 1)
            st.leave(HEADS)

            dve.wait_ge(s_mixhi, 1)
            dve.tensor_tensor(h[:, 0:8, 1, :], proj[:, AQ:AQ + 8, :], h[:, 0:8, 0, :].bitcast(F32), ALU.subtract).then_inc(s_mix, 1)
            dve.wait_ge(s_mixhi, 2)
            dve.tensor_tensor(h[:, 8:16, 1, :], proj[:, HG:HG + 8, :], h[:, 8:16, 0, :].bitcast(F32), ALU.subtract).then_inc(s_mix, 1)
            dve.wait_ge(s_mix, 2)
            dve.wait_ge(s_red, 5)
            for q in range(4):
                ins = dve.tensor_copy(g1b[:, q * UW:(q + 1) * UW], ps[4 + q][:, :])
                if q < 3:
                    st.do(ins)
            ins.then_inc(s_redc, 2)
            dve.wait_ge(s_redc, 4)
            st.wait()

            dve.wait_ge(s_xre, 16)
            ph = PH["out"]
            with dve.Fori(0, ph.groups) as i:
                st.enter(i, 2)
                pe0 = i * ph.pe_per + ph.pe0
                for j in range(1, 5):
                    lo_part(i * 4 + (ph.unit0 + j + 1), j % 2, pe0 + (j - 1))
                for b in range(TB):
                    cols = bass.ds(i * UW, UW)
                    dve.wait_ge(s_pe, pe0 + (3 + b + 1))
                    st.wait()
                    dve.tensor_tensor(ytmp[:], ps[2 + b][:, :], g1b[:, cols], ALU.mult).then_inc(s_evac, 1)
                    dve.wait_ge(s_evac, i * 2 + (ph.tile0 + b + 1 + 4))
                    st.do(dve.tensor_tensor(x1[:, b, cols], x1[:, b, cols], ytmp[:], ALU.add))
            st.leave(ph.groups)
            st.wait()
            dve.sem_inc(s_ms, 1)
            x_normed(xn, x1, 1).then_inc(s_xn, 1)
            h_tiles(1, lambda k: ps[4 + (k // 2) % 4][:, (k % 2) * SEQ:(k % 2 + 1) * SEQ], A2, B2,
                    lambda k: KT // 2 + k // 2 + 1)

            dve.wait_ge(s_spill, 16)
            dve.wait_ge(s_acc, 96)

            def ffn(name, group0):
                ph = PH[name]
                with dve.Fori(0, ph.groups // 2) as i:
                    st.enter(i, 23)
                    for half in range(2):
                        g = i * 2 + half
                        pe0 = g * ph.pe_per + ph.pe0
                        dst = up if half else gate
                        for j in range(1, 5):
                            lo_part(g * 4 + (ph.unit0 + j + 1), j % 2, pe0 + (j - 1))
                            if ph.ada and j % 2:
                                n = half * 2 + j // 2
                                dve.wait_ge(s_ada, i * 4 + (ph.ada0 + n + 2))
                                ada(acc_g2, None, n % 2, i * 32 + ((ph.ada0 + n) // 2 + 1) * 16, i * 4 + n)
                        for f in range(4):
                            st.wait()
                            channel_tile(ph, g, f, u[:])
                            dve.wait_ge(s_evac, g * 4 + (ph.tile0 + f + 1 + 4))

                            def w(tap):
                                return cw[:, bass.ds(i * 4 + (group0 * 4 + half * NF + tap * 88 + f), 1)]

                            st.then(dve.tensor_scalar(dst[:, f, :], u[:], w(2), cb[:, bass.ds(i * 4 + (group0 * 4 + half * NF + f), 1)],
                                                      ALU.mult, ALU.add))
                            st.then(dve.scalar_tensor_tensor(out=dst[:, f, 1:], in0=u[:, :SEQ - 1], scalar=w(1),
                                                             in1=dst[:, f, 1:], op0=ALU.mult, op1=ALU.add))
                            ins = dve.scalar_tensor_tensor(out=dst[:, f, 2:], in0=u[:, :SEQ - 2], scalar=w(0),
                                                           in1=dst[:, f, 2:], op0=ALU.mult, op1=ALU.add)
                            if half == 0 and f == 3:
                                ins.then_inc(s_convg, 1)
                            else:
                                st.do(ins)
                        if half == 0:
                            dve.wait_ge(s_convg, i + (group0 + 1))
                    st.wait()
                    dve.wait_ge(s_silu, i + (group0 + 1))
                    dve.tensor_tensor(up[:], up[:], gate[:], ALU.mult).then_inc(s_prod, 1)
                    dve.wait_ge(s_acthi, i + (group0 + 1))
                    dve.wait_ge(s_prod, i + (group0 + 1))
                    tiles = bass.ds(i * 4 + group0 * 4, 4)
                    dve.tensor_tensor(act_lo[:, tiles, :], up[:], act_hi[:, tiles, :].bitcast(F32), ALU.subtract).then_inc(s_h, 1)
                    dve.wait_ge(s_h, i + (2 * KT + group0 + 1))
                st.leave(ph.groups // 2)

            ffn("up_ada", 0)
            ffn("up", 4)

            ph = PH["down"]
            dve.wait_ge(s_pe, ph.pe0)
            dve.wait_ge(s_red, 6)
            for q in range(4):
                ins = dve.tensor_copy(g2b[:, q * UW:(q + 1) * UW], ps[4 + q][:, :])
                st.do(ins)
            st.wait()
            dve.wait_ge(s_xr, 32)
            for g in range(ph.groups):
                pe0 = ph.pe0 + g * ph.pe_per
                for j in range(1, ph.units + 1):
                    unit = ph.unit0 + g * ph.units + j
                    if unit < ph.unit0 + ph.groups * ph.units:
                        lo_part(unit + 1, unit % 2, pe0 + j - 1)
                for b in range(TB):
                    cols = slice(g * UW, (g + 1) * UW)
                    dve.wait_ge(s_pe, pe0 + ph.units - 1 + b + 1)
                    st.wait()
                    dve.tensor_tensor(junk2[:, 0:UW], ps[2 + b][:, :], g2b[:, cols], ALU.mult).then_inc(s_evac, 1)
                    dve.wait_ge(s_evac, ph.tile0 + g * 2 + b + 1 + 4)
                    st.do(dve.tensor_tensor(xr[:, b, cols], xr[:, b, cols], junk2[:, 0:UW], ALU.add))
            st.wait()
            dve.sem_inc(s_ms, 1)
            dve.wait_ge(s_rt, 3)
            st.then(dve.reciprocal(ss, rstd))
            for b in range(TB):
                dve.scalar_tensor_tensor(out=xr[:, b, :], in0=xr[:, b, :], scalar=ss[:, b:b + 1], in1=fnb[:],
                                         op0=ALU.mult, op1=ALU.mult).then_inc(s_fin, 1)


_INS = ["x", "c", "positions", "w_ada", "b_ada", "norm1_w", "w_in", "lb_logits", "gnorm_w", "w_out",
        "norm2_w", "w_up", "conv_w", "conv_b", "w_down", "final_norm_w"]


def kernel(**inputs):
    import numpy as _np
    import concourse.bacc as _bacc
    from concourse import mybir as _mybir
    from concourse.bass_utils import run_bass_kernel_spmd as _run

    nc = _bacc.Bacc("TRN2", target_bir_lowering=False, num_devices=1)
    arrays, args = {}, []
    f32, lv = constants()
    for name, a in [(n, _np.ascontiguousarray(inputs[n])) for n in _INS] + [("tab_f32", f32), ("tab_lv", lv)]:
        arrays[f"in_{name}"] = a
        args.append(nc.dram_tensor(f"in_{name}", a.shape, _mybir.dt.from_np(a.dtype), kind="ExternalInput").ap())
    args.append(nc.dram_tensor("out_0", (1, SEQ, D), _mybir.dt.float32, kind="ExternalOutput").ap())
    build(nc, *args)
    r = _run(nc, [arrays], core_ids=[0])
    return r.results[0]["out_0"]
```

```python
from contextlib import ExitStack

import numpy as np

import concourse.bass as bass
from concourse import mybir

F32 = mybir.dt.float32
F32R = mybir.dt.float32r
U8 = mybir.dt.uint8
I32 = mybir.dt.int32
ALU = mybir.AluOpType
ACT = mybir.ActivationFunctionType
AX = mybir.AxisListType

P = 128
SEQ, D, FF = 256, 2048, 5632
KT = D // P
TB = SEQ // P
HEADS, DH = 8, 128
ROT = DH // 4
LEVELS = 8
NF = FF // P
EPS = 1e-6
SCALE = DH ** -0.5
UW = 512
UK = 2
RING = 4
AHEAD = 3
AW = D // 2
HQ, HF, HG, AQ, AK = 0, 8, 16, 24, 32
SH1, SC1, G1, SH2, SC2, G2 = range(6)


class Phase:

    def __init__(self, kind, groups, units, ada, last):
        self.kind, self.groups, self.units, self.ada = kind, groups, units, ada
        self.tiles = 4 if kind == "channel" else 2
        self.unit0, self.tile0, self.pe0, self.ada0, self.chan0 = last
        self.pe_per = units - 1 + self.tiles

    def next(self):
        n = self.groups
        return (self.unit0 + n * self.units, self.tile0 + n * self.tiles, self.pe0 + n * self.pe_per,
                self.ada0 + n * self.ada, self.chan0 + n * self.tiles * (self.kind == "channel"))


def phases():
    at, out = (0, 0, 1, 2 * KT, 0), {}
    for name, kind, groups, units, ada in (
            ("hq_hf", "channel", 4, 8, 8), ("hi", "token", 2, 8, 8), ("hg", "channel", 2, 8, 8),
            ("aq_ak", "channel", 4, 8, 8), ("av", "token", 2, 8, 0), ("out", "token", 4, 8, 0),
            ("up", "channel", 22, 8, 0), ("down", "token", 4, 22, 0)):
        out[name] = Phase(kind, groups, units, ada, at)
        at = out[name].next()
        if name == "up":
            out["up"].ada_pairs = 8
            at = at[:3] + (at[3] + 32,) + at[4:]
    return out


class Group:

    def __init__(self, ph, n):
        self.units = ph.units
        self.unit0, self.tile0 = ph.unit0 + n * ph.units, ph.tile0 + n * ph.tiles


class Steps:

    def __init__(self, eng, sem):
        self.eng, self.sem, self.n, self.base = eng, sem, 0, 0

    def do(self, ins):
        ins.then_inc(self.sem, 1)
        self.n += 1

    def wait(self):
        self.eng.wait_ge(self.sem, self.base + self.n)

    def then(self, ins):
        self.do(ins)
        self.wait()

    def enter(self, i, per):
        self.start, self.per, self.base, self.n = self.n, per, self.n + i * per, 0

    def leave(self, times):
        assert self.n == self.per, (self.n, self.per)
        self.base, self.n = 0, self.start + times * self.per


def constants():
    t, s = np.arange(P)[:, None], np.arange(P)[None, :]

    def mult(d):
        return ((d >= 0) & (d <= 128)).astype(int) + ((d >= 0) & (d % 4 == 0)) + ((d >= 0) & (d % 16 == 0))

    m = np.concatenate([mult(t - s), mult(t - s + P), mult(t - s)], 1).astype(np.float32)
    neg = np.where(m > 0, 0, -1e30).astype(np.float32)
    rot = np.zeros((P, P), np.float32)
    for j in range(ROT // 2):
        rot[j + ROT // 2, j], rot[j, j + ROT // 2] = -1, 1
    freq = np.zeros((P, 1), np.float32)
    inv = (1.0 / (np.float32(500000.0) ** (np.arange(0, ROT, 2, dtype=np.float32) / np.float32(ROT)))).astype(np.float32)
    freq[:ROT, 0] = np.concatenate([inv, inv])
    f32 = np.concatenate([np.eye(P, dtype=np.float32), rot, neg, m, freq], 1)
    s, t = np.arange(P)[:, None], np.arange(P)[None, :]
    lv = [(s == t)] + [((s >> (l + 1)) == (t >> (l + 1))) & ((s >> l) % 2 == 0) & ((t >> l) % 2 == 1) for l in range(LEVELS - 1)]
    return f32, np.stack(lv, 1).reshape(P, LEVELS * P).astype(np.float32)


def build(nc, x, c, positions, w_ada, b_ada, norm1_w, w_in, lb_logits, gnorm_w, w_out,
          norm2_w, w_up, conv_w, conv_b, w_down, final_norm_w, tab_f32, tab_lv, out):
    PH = phases()
    w_in, w_out, w_up, w_down, w_ada = (w.rearrange("o k n -> (o k) n") for w in (w_in, w_out, w_up, w_down, w_ada))
    x_tok = x.rearrange("o (b p) d -> p (o b) d", p=P)
    out_tok = out.rearrange("o (b p) d -> p (o b) d", p=P)
    x1_dram = nc.dram_tensor("x1_spill", (P, TB, D), F32, kind="Internal").ap()

    with ExitStack() as ctx:
        names = {}

        def at(off, name, shape, dt=F32):
            return nc.alloc_sbuf_tensor_at(name, [P] + shape, dt, offset=BASE + off)

        def sem(name):
            names[name] = ctx.enter_context(nc.semaphore(name))
            return names[name]

        BASE = 16512
        K = 1024
        wraw = at(0, "wraw", [RING, UK, UW])
        araw = at(16 * K, "araw", [RING, AW])
        whi = at(32 * K, "whi", [RING, UK, UW], F32R)
        wlo = at(48 * K, "wlo", [RING, UK, UW], F32R)
        astart = at(32 * K, "astart", [RING, D])
        h = at(64 * K, "h", [KT, 2, SEQ], F32R)
        xr = at(64 * K, "xr", [TB, D])
        g2b = at(80 * K, "g2b", [D])
        fnb = at(88 * K, "fnb", [D])
        Z = 96 * K
        proj = at(Z, "proj", [40, SEQ])
        x0 = at(Z, "x0", [TB, D])
        xT = at(Z + 16 * K, "xT", [KT, SEQ])
        acc_b = at(Z + 32 * K, "acc_b", [D])
        x1 = at(Z, "x1", [TB, D])
        g1b = at(Z + 16 * K, "g1b", [D])
        xn = at(Z + 24 * K, "xn", [TB, D])
        vtok = at(Z + 40 * K, "vtok", [TB, 2 * HEADS * DH])
        rows = at(Z + 40 * K, "rows", [6, P])
        qp = at(Z + 56 * K, "qp", [LEVELS, SEQ])
        ks = at(Z + 64 * K, "ks", [LEVELS, SEQ])
        junk = at(Z + 56 * K, "junk", [D])
        htmp = at(Z + 64 * K, "htmp", [2, SEQ])
        ytmp = at(Z + 66 * K, "ytmp", [UW])
        tot = at(Z + 72 * K, "tot", [SEQ])
        aT = at(Z + 73 * K, "aT", [3, P])
        hv = at(Z + 75 * K, "hv", [TB, DH])
        osq = at(Z + 76 * K, "osq", [SEQ])
        orstd = at(Z + 77 * K, "orstd", [SEQ])
        onorm = at(Z + 78 * K, "onorm", [SEQ])
        aq = at(Z + 79 * K, "aq", [SEQ])
        avh = at(Z + 80 * K, "avh", [TB, DH])
        smask = at(Z + 81 * K, "smask", [3 * P])
        msk = at(Z + 81 * K, "msk", [LEVELS, P])
        prob = at(Z + 83 * K, "prob", [3 * P])
        probT = at(Z + 85 * K, "probT", [3 * P])
        cosr = at(Z + 87 * K, "cosr", [SEQ])
        sinr = at(Z + 88 * K, "sinr", [SEQ])
        rtmp = at(Z + 89 * K, "rtmp", [2, SEQ])
        acc = at(Z + 91 * K, "acc", [D])
        tab = at(Z + 99 * K, "tab", [7 * P + 1])
        lvm = at(Z + 103 * K, "lvm", [LEVELS, P], U8)
        act_hi = at(Z, "act_hi", [NF, SEQ], F32R)
        act_lo = at(Z + 44 * K, "act_lo", [NF, SEQ], F32R)
        gate = at(Z + 88 * K, "gate", [4, SEQ])
        up = at(Z + 92 * K, "up", [4, SEQ])
        acc_g2 = at(Z + 96 * K, "acc_g2", [D])
        junk2 = at(Z + 88 * K, "junk2", [D])
        Q = Z + 104 * K
        ident = at(Q, "ident", [P])
        ones = at(Q + 512, "ones", [P])
        evt = at(Z + 111 * K + 864 - 4 * K, "evt", [4, SEQ])
        NPRM = 65 + 4 * 88
        prm = at(Q + K, "prm", [NPRM])
        small = at(Q + K + 4 * NPRM + 28, "small", [192])
        assert Q + K + 4 * NPRM + 28 + 192 * 4 <= Z + 107 * K + 864 and BASE + Z + 111 * K + 864 <= 229368
        rot, neg, mult, freq = tab[:, 0:P], tab[:, P:4 * P], tab[:, 4 * P:7 * P], tab[:, 7 * P:7 * P + 1]
        n1w, n2w, lbl = prm[:, 16:32], prm[:, 32:48], prm[:, 48:64]
        gn = prm[:, 64:65]
        cw, cb = prm[:, 65:65 + 264], prm[:, 65 + 264:65 + 352]
        csilu = small[:, 0:16]
        A1, B1, A2, B2 = (small[:, 16 + 16 * j:32 + 16 * j] for j in range(4))
        lb, one_lb, lbm = small[:, 80:88], small[:, 88:96], small[:, 96:104]
        lbe = small[:, 104:120]
        ss, rstd = small[:, 120:122], small[:, 122:124]
        mx, den = small[:, 124:126], small[:, 126:128]
        rden = small[:, 128:130]
        epsc, scratch = small[:, 130:131], small[:, 131:132]

        bank = ctx.enter_context(nc.psum_tensor("bank", [P, 8, 512], F32))
        ps = [bank[:, b, :] for b in range(8)]

        s_in = sem("s_in")
        s_inc = sem("s_inc")
        s_cst = sem("s_cst")
        s_lvm = sem("s_lvm")
        s_x = sem("s_x")
        s_xre = sem("s_xre")
        s_w = [sem(f"s_w{j}") for j in range(RING)]
        s_as = [sem(f"s_as{j}") for j in range(RING)]
        s_a = [sem(f"s_a{j}") for j in range(RING)]
        s_hi = sem("s_hi")
        s_lo = sem("s_lo")
        s_ada = sem("s_ada")
        s_pe = sem("s_pe")
        s_evt = sem("s_evt")
        s_evac = sem("s_evac")
        s_acc = sem("s_acc")
        s_accz = sem("s_accz")
        s_red = sem("s_red")
        s_redc = sem("s_redc")
        s_v = sem("s_v")
        s_s = sem("s_s")
        s_p = sem("s_p")
        s_prmT = sem("s_prmT")
        s_prm = sem("s_prm")
        s_csilu = sem("s_csilu")
        s_lbd = sem("s_lbd")
        s_lbe = sem("s_lbe")
        s_sq = sem("s_sq")
        s_ms = sem("s_ms")
        s_rt = sem("s_rt")
        s_xn = sem("s_xn")
        s_xT = sem("s_xT")
        s_xTc = sem("s_xTc")
        s_ht = sem("s_ht")
        s_hhi = sem("s_hhi")
        s_h = sem("s_h")
        s_ang = sem("s_ang")
        s_cs = sem("s_cs")
        s_gates = sem("s_gates")
        s_f = sem("s_f")
        s_rotP = sem("s_rotP")
        s_rotU = sem("s_rotU")
        s_rope = sem("s_rope")
        s_hv = sem("s_hv")
        s_lvA = sem("s_lvA")
        s_lvB = sem("s_lvB")
        s_lvC = sem("s_lvC")
        s_scA = sem("s_scA")
        s_scB = sem("s_scB")
        s_mA = sem("s_mA")
        s_mB = sem("s_mB")
        s_aT = sem("s_aT")
        s_cross = sem("s_cross")
        s_crossC = sem("s_crossC")
        s_oT = sem("s_oT")
        s_osq = sem("s_osq")
        s_oss = sem("s_oss")
        s_orstd = sem("s_orstd")
        s_hdone = sem("s_hdone")
        s_aqv = sem("s_aqv")
        s_S = sem("s_S")
        s_smask = sem("s_smask")
        s_smax = sem("s_smax")
        s_prob = sem("s_prob")
        s_pn = sem("s_pn")
        s_pT = sem("s_pT")
        s_pTc = sem("s_pTc")
        s_ao = sem("s_ao")
        s_aoc = sem("s_aoc")
        s_mixhi = sem("s_mixhi")
        s_mix = sem("s_mix")
        s_spill = sem("s_spill")
        s_silu = sem("s_silu")
        s_convg = sem("s_convg")
        s_convu = sem("s_convu")
        s_acthi = sem("s_acthi")
        s_xr = sem("s_xr")
        s_prod = sem("s_prod")
        s_pn0 = sem("s_pn0")
        s_fin = sem("s_fin")
        s_out = sem("s_out")

        block = ctx.enter_context(nc.Block())

        @block.sync
        def _(sp):
            def load_unit(w, unit, slot, k0, col):
                sp.wait_ge(s_lo, unit + 1)
                src = w[k0:k0 + UK * P, bass.ds(col, UW)].rearrange("(k p) n -> p k n", p=P)
                sp.dma_start(wraw[:, slot], src).then_inc(s_w[slot], 16)

            def load_ada(number, slot, mod, row, half):
                sp.wait_ge(s_ada, number + 1)
                src = w_ada[bass.ds(row, P), mod * D + half * AW:mod * D + (half + 1) * AW]
                sp.dma_start(araw[:, slot], src).then_inc(s_a[slot], 16)

            with sp.Fori(0, KT // 2) as r:
                for n, (mod, row) in enumerate(((SH1, 0), (SC1, 0), (SH1, 1), (SC1, 1))):
                    sp.wait_ge(s_ada, r * 4 + (n + 1))
                    sp.dma_start(astart[:, n], w_ada[bass.ds(r * (2 * P) + row * P, P), mod * D:(mod + 1) * D]).then_inc(s_as[n], 16)

            def phase(name, w, col0, mod=None, row0=0):
                ph = PH[name]
                with sp.Fori(0, ph.groups) as i:
                    for j in range(ph.units):
                        load_unit(w, i * ph.units + (ph.unit0 + j), j % RING, j * UK * P, i * UW + col0)
                        if ph.ada:
                            load_ada(i * 8 + (ph.ada0 + j), j % RING, mod, i * (4 * P) + (row0 + j // 2) * P, j % 2)

            phase("hq_hf", w_in, 3072, SH2)
            phase("hi", w_in, 5120, SC2)
            phase("hg", w_in, 6144, SC2, 8)
            phase("aq_ak", w_in, 0, G1)
            phase("av", w_in, 2048)
            phase("out", w_out, 0)

            ph = PH["up"]

            def pairs(first, last, ada):
                with sp.Fori(first, last) as i:
                    for half in range(2):
                        for j in range(8):
                            load_unit(w_up, i * 16 + (ph.unit0 + half * 8 + j), j % RING, j * UK * P, i * UW + half * FF)
                            if ada and j % 4 == 1:
                                n = half * 2 + j // 4
                                load_ada(i * 4 + (ph.ada0 + n), n, G2, i * (2 * P) + n // 2 * P, n % 2)

            pairs(0, ph.ada_pairs, True)
            pairs(ph.ada_pairs, ph.groups // 2, False)
            ph = PH["down"]
            with sp.Fori(0, ph.groups // 2) as i:
                for half in range(2):
                    for j in range(ph.units):
                        n = half * ph.units + j
                        load_unit(w_down, i * (2 * ph.units) + (ph.unit0 + n), n % RING, j * UK * P, i * (2 * UW) + half * UW)
            sp.wait_ge(s_fin, TB)
            sp.dma_start(out_tok, xr[:]).then_inc(s_out, 16)
            sp.wait_ge(s_out, 16)

        @block.gpsimd
        def _(gp):
            st = Steps(gp, s_p)
            gp.memset(ones[:], 1.0).then_inc(s_cst, 1)
            gp.memset(epsc, EPS).then_inc(s_cst, 1)
            def init_acc(a, mod):
                st.then(gp.memset(a[:], 0.0))
                gp.dma_start(a[0:1, :], b_ada[:, mod * D:(mod + 1) * D]).then_inc(s_acc, 16)

            init_acc(acc, SH1)
            init_acc(acc_b, SC1)
            for t in range(3):
                gp.dma_start(rows[0:88, 1 + t, :], conv_w[0, t].rearrange("(r p) -> r p", p=P)).then_inc(s_in, 16)
            gp.dma_start(rows[0:88, 4, :], conv_b.rearrange("o (r p) -> (o r) p", p=P)).then_inc(s_in, 16)
            gp.dma_start(tab[:], tab_f32[:, P:]).then_inc(s_in, 16)
            gp.dma_start(msk[:].rearrange("p l t -> p (l t)"), tab_lv).then_inc(s_in, 16)
            gp.dma_start(rtmp[0:ROT, 0, :].bitcast(I32), positions.to_broadcast([ROT, SEQ])).then_inc(s_in, 16)

            gp.wait_ge(s_in, 7 * 16)
            gp.tensor_copy(lvm[:], msk[:]).then_inc(s_lvm, 1)

            for red, mod in ((8, SH2), (9, SC2), (10, G1)):
                gp.wait_ge(s_red, red)
                init_acc(acc, mod)
            gp.wait_ge(s_evac, PH["hg"].tile0 + 4)
            with gp.Fori(0, HEADS) as hd:
                gp.wait_ge(s_oT, hd + 1)
                gp.tensor_copy(hv[:], vtok[:, :, bass.ds(hd * DH, DH)]).then_inc(s_hv, 1)
            gp.wait_ge(s_evac, PH["out"].tile0 + 4)
            gp.wait_ge(s_rope, 1)
            with gp.Fori(0, HEADS) as hd:
                gp.wait_ge(s_ao, hd + 1)
                gp.tensor_copy(aq[:], proj[:, bass.ds(hd + AQ, 1), :].rearrange("p a t -> p (a t)")).then_inc(s_aqv, 1)
                gp.tensor_copy(avh[:], vtok[:, :, bass.ds(hd * DH + HEADS * DH, DH)]).then_inc(s_aqv, 1)
            gp.wait_ge(s_mix, 2)
            gp.dma_start(x1[:], x_tok).then_inc(s_xre, 16)
            gp.wait_ge(s_h, 2 * KT)
            gp.dma_start(x1_dram, x1[:]).then_inc(s_spill, 16)
            init_acc(acc_g2, G2)
            gp.wait_ge(s_spill, 16)
            gp.wait_ge(s_pe, PH["down"].pe0)
            gp.dma_start(xr[:], x1_dram).then_inc(s_xr, 16)
            gp.dma_start(fnb[:], final_norm_w.rearrange("(o d) -> o d", o=1).to_broadcast([P, D])).then_inc(s_xr, 16)

        @block.scalar
        def _(act):
            st = Steps(act, s_s)
            for start in (s_aoc,):
                act.sem_inc(start, 1)

            r0 = 0
            for src in (c.rearrange("o (r p) -> (o r) p", p=P), norm1_w.rearrange("o (r p) -> (o r) p", p=P),
                        norm2_w.rearrange("o (r p) -> (o r) p", p=P), lb_logits.rearrange("o (r p) -> (o r) p", p=P),
                        gnorm_w):
                n = src.shape[0]
                act.dma_start(rows[r0:r0 + n, 0, :], src).then_inc(s_inc, 16)
                r0 += n
            act.dma_start(ident[:], tab_f32[:, 0:P]).then_inc(s_inc, 16)
            act.dma_start(x0[:], x_tok).then_inc(s_x, 16)

            def hi_part(slot, count, ready=None):
                act.wait_ge(s_w[slot], count)
                if ready is not None:
                    act.wait_ge(s_pe, ready)
                act.activation(whi[:, slot], wraw[:, slot], ACT.Copy).then_inc(s_hi, 1)

            def hi_ahead(unit0, units, i, j, pe0, loads):
                hi_part((unit0 + j) % RING, i * loads + ((unit0 + j) // RING + 1) * 16, pe0 + (j - AHEAD))

            def lo_columns(pair):
                act.activation(evt[:, 2 * pair:2 * pair + 2], bank[:, 2 * pair:2 * pair + 2, 256:512], ACT.Copy).then_inc(s_evt, 1)

            def stream(name):
                ph = PH[name]
                n = ph.units
                with act.Fori(0, ph.groups) as i:
                    pe0 = i * ph.pe_per + ph.pe0
                    for j in range(AHEAD, n + AHEAD):
                        if j == n + AHEAD - 1 and ph.kind == "channel":
                            for pair in range(2):
                                act.wait_ge(s_pe, pe0 + (n - 1 + 2 * pair + 2))
                                act.wait_ge(s_evac, i * 4 + (ph.tile0 + 2 * pair - 2 + 4))
                                lo_columns(pair)
                        hi_ahead(ph.unit0, n, i, j, pe0, n // RING * 16)

            act.wait_ge(s_prm, 1)
            act.activation(csilu, prm[:, 0:16], ACT.Silu).then_inc(s_csilu, 1)
            act.wait_ge(s_lbd, 1)
            act.activation(lbe, lbe, ACT.Exp).then_inc(s_lbe, 1)

            def norm_sums(src, scratch, n):
                for b in range(TB):
                    if b:
                        st.wait()
                    st.do(act.activation(scratch[:], src[:, b, :], ACT.Square, accum_out=ss[:, b:b + 1]))
                st.wait()
                act.activation(rstd, ss, ACT.Sqrt, bias=epsc, scale=1.0 / D).then_inc(s_rt, 1)

            act.wait_ge(s_x, 16)
            act.wait_ge(s_cst, 2)
            norm_sums(x0, junk, 0)
            for k in range(KT // 2):
                act.wait_ge(s_xT, k + 1)
                act.activation(xT[:, 2 * k:2 * k + 2, :], ps[4 + k % 4][:, :].rearrange("p (a t) -> p a t", a=2),
                               ACT.Copy).then_inc(s_xTc, 1)
            act.wait_ge(s_ang, 1)
            act.activation(sinr[0:ROT], sinr[0:ROT], ACT.Sin).then_inc(s_cs, 1)
            act.activation(cosr[0:ROT], cosr[0:ROT], ACT.Sin).then_inc(s_cs, 1)
            def h_hi(n):
                for k in range(KT):
                    act.wait_ge(s_ht, n * KT + k + 1)
                    act.activation(h[:, k, 0, :], htmp[:, k % 2], ACT.Copy).then_inc(s_hhi, 1)
                    if n == 0 and k % 2 and k // 2 < AHEAD:
                        act.wait_ge(s_ada, 2 * KT + 4)
                        hi_part(k // 2, 16)

            h_hi(0)
            stream("hq_hf")
            stream("hi")
            stream("hg")
            stream("aq_ak")
            stream("av")

            act.wait_ge(s_evac, PH["aq_ak"].tile0 + 4)
            act.activation(proj[:, HQ:HQ + 8, :], proj[:, HQ:HQ + 8, :], ACT.Silu).then_inc(s_gates, 1)
            act.activation(proj[:, HG:HG + 8, :], proj[:, HG:HG + 8, :], ACT.Silu).then_inc(s_gates, 1)
            act.activation(proj[:, HF:HF + 8, :], proj[:, HF:HF + 8, :], ACT.Sigmoid).then_inc(s_gates, 1)
            with act.Fori(0, HEADS) as hd:
                act.wait_ge(s_cross, hd + 2)
                act.activation(aT[:, 1, :], ps[4][:, 0:P], ACT.Copy).then_inc(s_crossC, 1)
                act.wait_ge(s_oT, hd + 2)
                act.activation(osq[:], ps[5][:, 0:SEQ], ACT.Square).then_inc(s_osq, 1)
                act.wait_ge(s_oss, hd + 1)
                act.wait_ge(s_hdone, hd + 1)
                act.activation(orstd[:], ps[6][:, 0:SEQ], ACT.Sqrt, bias=epsc, scale=1.0 / DH).then_inc(s_orstd, 1)
            with act.Fori(0, HEADS) as hd:
                act.wait_ge(s_smax, hd + 1)
                act.activation(prob[:, 0:P], smask[:, 0:P], ACT.Exp, bias=mx[:, 0:1], scale=SCALE).then_inc(s_prob, 1)
                act.activation(prob[:, P:], smask[:, P:], ACT.Exp, bias=mx[:, 1:2], scale=SCALE).then_inc(s_prob, 1)
                act.wait_ge(s_pT, hd + 2)
                act.activation(probT[:], ps[5][:, 0:3 * P], ACT.Copy).then_inc(s_pTc, 1)
                act.wait_ge(s_ao, hd + 2)
                act.activation(proj[:, bass.ds(hd + AQ, 1), :].rearrange("p a t -> p (a t)"), ps[6][:, 0:SEQ],
                               ACT.Copy).then_inc(s_aoc, 1)
            act.wait_ge(s_aoc, HEADS + 1)
            act.wait_ge(s_hdone, HEADS + 1)
            act.activation(h[:, 0:8, 0, :], proj[:, AQ:AQ + 8, :], ACT.Copy).then_inc(s_mixhi, 1)
            act.activation(h[:, 8:16, 0, :], proj[:, HG:HG + 8, :], ACT.Copy).then_inc(s_mixhi, 1)
            stream("out")

            act.wait_ge(s_evac, PH["up"].tile0 + 4)
            act.wait_ge(s_ms, 1)
            norm_sums(x1, junk, 1)
            h_hi(1)

            ph = PH["up"]

            def ffn_half(i, half, finished):
                pe0 = (i * 2 + half) * ph.pe_per + ph.pe0
                banks = bank[:, 4 - 4 * half:8 - 4 * half, 256:512]
                for j in range(AHEAD, 8 + AHEAD):
                    hi_ahead(ph.unit0 + half * 8, 8, i, j, pe0, 64)
                    if j == AHEAD and finished:
                        if half:
                            act.wait_ge(s_convu, i + 1)
                        else:
                            act.wait_ge(s_convg, i)
                        act.activation(evt[:], banks, ACT.Copy).then_inc(s_evt, 1)
                    if j == AHEAD + 5:
                        if half:
                            act.wait_ge(s_convg, i + 1)
                            act.activation(gate[:], gate[:], ACT.Silu).then_inc(s_silu, 1)
                        elif finished:
                            act.wait_ge(s_prod, i)
                            act.activation(act_hi[:, bass.ds(i * 4 - 4, 4), :], up[:], ACT.Copy).then_inc(s_acthi, 1)

            ffn_half(0, 0, False)
            ffn_half(0, 1, True)
            with act.Fori(1, ph.groups // 2) as i:
                ffn_half(i, 0, True)
                ffn_half(i, 1, True)
            ph = PH["down"]
            for g in range(ph.groups):
                for j in range(AHEAD, ph.units + AHEAD):
                    unit = ph.unit0 + g * ph.units + j
                    if unit < ph.unit0 + ph.groups * ph.units:
                        hi_part(unit % RING, (unit // RING + 1) * 16, ph.pe0 + g * ph.pe_per + j - AHEAD)
                    if g == 0 and j == AHEAD:
                        act.wait_ge(s_convg, 11)
                        act.activation(evt[:], bank[:, 4:8, 256:512], ACT.Copy).then_inc(s_evt, 1)
                    if g == 0 and j == AHEAD + 5:
                        act.wait_ge(s_prod, 11)
                        act.activation(act_hi[:, NF - 4:, :], up[:], ACT.Copy).then_inc(s_acthi, 1)
            act.wait_ge(s_ms, 2)
            norm_sums(xr, junk2, 2)

        @block.tensor
        def _(pe):
            for start in (s_pe, s_oT, s_cross, s_ao, s_pT):
                pe.sem_inc(start, 1)
            pe.wait_ge(s_inc, 6 * 16)
            pe.transpose(ps[0][:, 0:65], rows[0:65, 0, :], ident[0:65, 0:65]).then_inc(s_prmT, 1)
            pe.wait_ge(s_in, 7 * 16)
            pe.wait_ge(s_prm, 1)
            for t in range(4):
                last = pe.transpose(ps[0][:, 65 + 88 * t:65 + 88 * (t + 1)], rows[0:88, 1 + t, :], ident[0:88, 0:88])
            last.then_inc(s_prmT, 1)

            def x_transposes(src, n):
                for k in range(KT // 2):
                    if k >= 4:
                        if n == 0:
                            pe.wait_ge(s_xTc, k - 3)
                        else:
                            pe.wait_ge(s_ht, KT + 2 * (k - 3))
                    for a in range(2):
                        for b in range(TB):
                            last = pe.transpose(ps[4 + k % 4][:, a * SEQ + b * P:a * SEQ + (b + 1) * P],
                                                src[:, b, (2 * k + a) * P:(2 * k + a + 1) * P], ident[:])
                    last.then_inc(s_xT, 1)

            pe.wait_ge(s_xn, 1)
            x_transposes(x0, 0)

            def mod_columns(a, col, k0=0, k1=KT, bank0=7):
                for k in range(k0, k1):
                    last = pe.matmul(ps[bank0][:, col + k:col + k + 1], a[:, k * P:(k + 1) * P], ones[:, 0:1],
                                     start=True, stop=True)
                last.then_inc(s_red, 1)

            def channel_group(ph, i, h_done, bank0=0, reuse=4, between=None):
                for j in range(ph.units):
                    slot = (ph.unit0 + j) % RING
                    pe.wait_ge(s_lo, i * ph.units + (ph.unit0 + j + 1 + 4))
                    pe.wait_ge(s_h, h_done + UK * (j + 1))
                    for f in range(4):
                        out = ps[bank0 + f]
                        if j == 0:
                            pe.wait_ge(s_evac, i * 4 + (ph.tile0 + f - reuse + 1 + 4))
                        cols = slice(f * P, (f + 1) * P)
                        for k in range(UK):
                            kk = j * UK + k
                            pe.matmul(out, whi[:, slot, k, cols], h[:, kk].rearrange("p a t -> p (a t)"),
                                      start=(kk == 0), stop=False, skip_group_check=True)
                            last = pe.matmul(out[:, 0:SEQ], wlo[:, slot, k, cols], h[:, kk, 0, :],
                                             start=False, stop=(kk == KT - 1), skip_group_check=True)
                        if j == ph.units - 1:
                            last.then_inc(s_pe, 1)
                    if j < ph.units - 1:
                        last.then_inc(s_pe, 1)
                    if between:
                        between(j)

            def token_group(ph, i, hi, lo, unit0=None, bank0=2, reuse=2, ready=None):
                for j in range(ph.units):
                    slot = (ph.unit0 + j) % RING if unit0 is None else (unit0 + j) % RING
                    pe.wait_ge(s_lo, i * ph.units + (ph.unit0 + j + 1 + 4))
                    if ready:
                        pe.wait_ge(s_h, ready(j))
                    for b in range(TB):
                        if j == 0:
                            pe.wait_ge(s_evac, i * 2 + (ph.tile0 + b - reuse + 1 + 4))
                        for k in range(UK):
                            kk = j * UK + k
                            first, end = kk == 0, kk == ph.units * UK - 1
                            pe.matmul(ps[bank0 + b], hi(kk, b), whi[:, slot, k, :], start=first, stop=False)
                            pe.matmul(ps[bank0 + b], hi(kk, b), wlo[:, slot, k, :], start=False, stop=False)
                            last = pe.matmul(ps[bank0 + b], lo(kk, b), whi[:, slot, k, :], start=False, stop=end)
                        if j == ph.units - 1:
                            last.then_inc(s_pe, 1)
                    if j < ph.units - 1:
                        last.then_inc(s_pe, 1)

            def h_hi(k, b):
                return h[:, k, 0, b * P:(b + 1) * P]

            def h_lo(k, b):
                return h[:, k, 1, b * P:(b + 1) * P]

            pe.wait_ge(s_ada, 2 * KT + 4)
            pe.wait_ge(s_xTc, KT // 2)
            pe.wait_ge(s_prm, 2)

            def first_columns(q):
                mod_columns(acc, 0, 4 * q, 4 * q + 4, 4 + q)
                mod_columns(acc_b, KT, 4 * q, 4 * q + 4, 4 + q)

            first_columns(0)
            first_columns(1)
            channel_group(PH["hq_hf"], 0, 0, between=lambda j: first_columns(2 + j // 2) if j in (0, 2) else None)
            with pe.Fori(1, PH["hq_hf"].groups) as i:
                channel_group(PH["hq_hf"], i, 0)
            pe.wait_ge(s_ada, PH["hi"].ada0 + 4)
            pe.wait_ge(s_redc, 4)
            mod_columns(acc, 0)
            with pe.Fori(0, PH["hi"].groups) as i:
                token_group(PH["hi"], i, h_hi, h_lo)
            with pe.Fori(0, PH["hg"].groups) as i:
                channel_group(PH["hg"], i, 0)
            pe.wait_ge(s_ada, PH["aq_ak"].ada0 + 4)
            mod_columns(acc, KT)
            with pe.Fori(0, PH["aq_ak"].groups) as i:
                channel_group(PH["aq_ak"], i, 0)
            with pe.Fori(0, PH["av"].groups) as i:
                token_group(PH["av"], i, h_hi, h_lo)

            pe.wait_ge(s_f, 1)
            pe.wait_ge(s_redc, 5)
            with pe.Fori(0, HEADS) as hd:
                q_h = proj[:, bass.ds(hd + HQ, 1), :].rearrange("p a t -> p (a t)")
                pe.wait_ge(s_lvA, hd + 1)
                pe.wait_ge(s_hdone, hd + 1)
                for b in range(TB):
                    tok = slice(b * P, (b + 1) * P)
                    pe.matmul(ps[4 + b][:, 0:P], ks[:, 0, tok], q_h[:, tok], start=True, stop=True)
                    for l in range(3):
                        last = pe.matmul(ps[4 + b][:, (l + 1) * P:(l + 2) * P], ks[:, l, tok], qp[:, l, tok],
                                         start=True, stop=True)
                last.then_inc(s_scA, 1)
                pe.wait_ge(s_lvB, hd + 1)
                for b in range(TB):
                    tok = slice(b * P, (b + 1) * P)
                    for l in range(3, 7):
                        last = pe.matmul(ps[6 + b][:, (l - 3) * P:(l - 2) * P], ks[:, l, tok], qp[:, l, tok],
                                         start=True, stop=True)
                last.then_inc(s_scB, 1)
                pe.wait_ge(s_lvC, hd + 1)
                pe.wait_ge(s_mA, hd + 1)
                pe.matmul(ps[4][:, 0:P], ks[:, 7, 0:P], qp[:, 7, P:SEQ], start=True, stop=True).then_inc(s_cross, 1)
                pe.wait_ge(s_aT, hd + 1)
                pe.wait_ge(s_crossC, hd + 1)
                pe.wait_ge(s_hv, hd + 1)
                pe.matmul(ps[5][:, 0:SEQ], hv[:, 0, :], aT[:, 0:2, :].rearrange("p a t -> p (a t)"),
                          start=True, stop=False, skip_group_check=True)
                pe.matmul(ps[5][:, P:SEQ], hv[:, 1, :], aT[:, 2, :], start=False, stop=True,
                          skip_group_check=True).then_inc(s_oT, 1)
                pe.wait_ge(s_osq, hd + 1)
                pe.matmul(ps[6][:, 0:SEQ], ones[:], osq[:], start=True, stop=True).then_inc(s_oss, 1)

            pe.wait_ge(s_evac, PH["av"].tile0 + 4)
            pe.wait_ge(s_hdone, HEADS + 1)
            with pe.Fori(0, 8) as j:
                pe.wait_ge(s_rotU, j + 1)
                pe.matmul(ps[7][:, :], rot, proj[:, bass.ds(j * 2 + AQ, 2), :].rearrange("p a t -> p (a t)"),
                          start=True, stop=True).then_inc(s_rotP, 1)

            with pe.Fori(0, HEADS) as hd:
                k_h = proj[:, bass.ds(hd + AK, 1), :].rearrange("p a t -> p (a t)")
                pe.wait_ge(s_aqv, hd * 2 + 2)
                pe.wait_ge(s_smask, hd + 1)
                pe.matmul(ps[4][:, 0:P], aq[:, 0:P], k_h[:, 0:P], start=True, stop=True)
                pe.matmul(ps[4][:, P:3 * P], aq[:, P:SEQ], k_h, start=True, stop=True).then_inc(s_S, 1)
                pe.wait_ge(s_pn, hd + 1)
                for t in range(3):
                    last = pe.transpose(ps[5][:, t * P:(t + 1) * P], prob[:, t * P:(t + 1) * P], ident[:])
                last.then_inc(s_pT, 1)
                pe.wait_ge(s_pTc, hd + 1)
                pe.wait_ge(s_aoc, hd + 1)
                pe.matmul(ps[6][:, 0:SEQ], avh[:, 0, :], probT[:, 0:SEQ], start=True, stop=False, skip_group_check=True)
                pe.matmul(ps[6][:, P:SEQ], avh[:, 1, :], probT[:, SEQ:], start=False, stop=True,
                          skip_group_check=True).then_inc(s_ao, 1)

            def mod_row(a, banks):
                for q in range(4):
                    last = pe.matmul(ps[banks[q]][:, :], ones[:], a[:, q * UW:(q + 1) * UW], start=True, stop=True)
                last.then_inc(s_red, 1)

            pe.wait_ge(s_ada, PH["av"].ada0 + 4)
            pe.wait_ge(s_aoc, HEADS + 1)
            mod_row(acc, (4, 5, 6, 7))
            pe.wait_ge(s_mix, 2)
            with pe.Fori(0, PH["out"].groups) as i:
                token_group(PH["out"], i, h_hi, h_lo)

            pe.wait_ge(s_xn, 2)
            pe.wait_ge(s_redc, 7)
            x_transposes(xn, 1)
            ph = PH["up"]
            with pe.Fori(0, ph.groups // 2) as i:
                for half in range(2):
                    pe_group = Group(ph, half)
                    channel_group(pe_group, i * 2, KT, 4 * half, 8)
            pe.wait_ge(s_ada, PH["down"].ada0 + 4)
            pe.wait_ge(s_evac, PH["down"].tile0 - 4 + 4)
            mod_row(acc_g2, (0, 1, 2, 3))
            ph = PH["down"]
            for g in range(ph.groups):
                if g == 2:
                    pe.wait_ge(s_redc, 8)
                token_group(ph, g, lambda k, b: act_hi[:, k, b * P:(b + 1) * P], lambda k, b: act_lo[:, k, b * P:(b + 1) * P],
                            ph.unit0 + g * ph.units, (4, 6, 0, 2)[g], 2 if g == 0 else 6,
                            lambda j: 2 * KT + (UK * j) // 4 + 1)

        @block.vector
        def _(dve):
            st = Steps(dve, s_v)
            for start in (s_hdone, s_smask, s_rotU):
                dve.sem_inc(start, 1)
            dve.sem_inc(s_convu, 1)
            dve.sem_inc(s_lo, RING)
            dve.sem_inc(s_ada, RING)
            dve.sem_inc(s_evac, 4)

            dve.wait_ge(s_prmT, 1)
            dve.tensor_copy(prm[:, 0:65], ps[0][:, 0:65]).then_inc(s_prm, 1)
            dve.wait_ge(s_prm, 1)
            st.then(dve.tensor_tensor(lbm, lbl[:, 0:8], lbl[:, 8:16], ALU.max))
            st.do(dve.tensor_tensor(lbe[:, 0:8], lbl[:, 0:8], lbm, ALU.subtract))
            dve.tensor_tensor(lbe[:, 8:16], lbl[:, 8:16], lbm, ALU.subtract).then_inc(s_lbd, 1)
            dve.wait_ge(s_lbe, 1)
            st.then(dve.tensor_tensor(lbm, lbe[:, 0:8], lbe[:, 8:16], ALU.add))
            st.then(dve.reciprocal(lbm, lbm))
            st.then(dve.tensor_tensor(lb, lbe[:, 0:8], lbm, ALU.mult))
            st.then(dve.tensor_scalar(one_lb, lb, -1.0, 1.0, ALU.mult, ALU.add))

            def x_normed(dst, src, n):
                dve.wait_ge(s_rt, n + 1)
                st.then(dve.reciprocal(ss, rstd))
                st.do(dve.tensor_scalar(dst[:, 0, :], src[:, 0, :], ss[:, 0:1], None, ALU.mult))
                dve.wait_ge(s_v, st.n)
                return dve.tensor_scalar(dst[:, 1, :], src[:, 1, :], ss[:, 1:2], None, ALU.mult)

            x_normed(x0, x0, 0).then_inc(s_xn, 1)

            def ada(a, number, slot, count, row):
                dve.wait_ge(s_a[slot], count)
                dve.scalar_tensor_tensor(out=a[:], in0=araw[:, slot], scalar=csilu[:, bass.ds(row, 1)], in1=a[:],
                                         op0=ALU.mult, op1=ALU.add).then_inc(s_ada, 1)

            dve.wait_ge(s_acc, 32)
            dve.wait_ge(s_csilu, 1)
            with dve.Fori(0, KT // 2) as r:
                for n in range(4):
                    a = (acc, acc_b)[n % 2]
                    dve.wait_ge(s_as[n], r * 16 + 16)
                    dve.wait_ge(s_ada, r * 4 + (n - 1 + 4))
                    dve.scalar_tensor_tensor(out=a[:], in0=astart[:, n], scalar=csilu[:, bass.ds(r * 2 + n // 2, 1)],
                                             in1=a[:], op0=ALU.mult, op1=ALU.add).then_inc(s_ada, 1)

            def ada(a, mine, slot, count, row, half):
                dve.wait_ge(s_a[slot], count)
                dve.wait_ge(s_ada, mine)
                cols = slice(half * AW, (half + 1) * AW)
                dve.scalar_tensor_tensor(out=a[:, cols], in0=araw[:, slot], scalar=csilu[:, bass.ds(row, 1)],
                                         in1=a[:, cols], op0=ALU.mult, op1=ALU.add).then_inc(s_ada, 1)

            dve.wait_ge(s_prmT, 2)
            dve.tensor_copy(prm[:, 65:], ps[0][:, 65:NPRM]).then_inc(s_prm, 1)

            posf, ang, turns, wrap = rtmp[0:ROT, 0, :], sinr[0:ROT], cosr[0:ROT], rtmp[0:ROT, 1, :]
            MAGIC = 1.5 * 2 ** 23
            T1 = 6.28125
            T2 = float(np.float32(np.round((2 * np.pi - T1) * 2 ** 20) / 2 ** 20))
            T3 = 2 * np.pi - T1 - T2
            dve.wait_ge(s_in, 7 * 16)
            st.then(dve.tensor_copy(wrap, posf.bitcast(I32)))
            st.then(dve.tensor_scalar(ang, wrap, freq[0:ROT], None, ALU.mult))
            st.then(dve.tensor_scalar(turns, ang, 1.0 / (2 * np.pi), MAGIC, ALU.mult, ALU.add))
            st.then(dve.tensor_scalar(turns, turns, -MAGIC, None, ALU.add))
            for part in (T1, T2, T3):
                st.then(dve.scalar_tensor_tensor(out=ang, in0=turns, scalar=-part, in1=ang, op0=ALU.mult, op1=ALU.add))
            PI = float(np.float32(3.1415925))
            st.then(dve.tensor_scalar(ang, ang, PI, -PI, ALU.min, ALU.max))
            st.then(dve.tensor_scalar(turns, ang, np.pi / 2, None, ALU.add))
            st.then(dve.tensor_scalar(wrap, turns, PI, -2 * np.pi, ALU.is_gt, ALU.mult))
            st.then(dve.tensor_tensor(turns, turns, wrap, ALU.add))
            dve.tensor_scalar(turns, turns, PI, -PI, ALU.min, ALU.max).then_inc(s_ang, 1)

            def first_columns(q):
                cols = slice(4 * q, 4 * q + 4)
                dve.wait_ge(s_red, 2 * q + 2)
                st.do(dve.tensor_copy(B1[:, cols], ps[4 + q][:, 4 * q:4 * q + 4]))
                dve.scalar_tensor_tensor(out=A1[:, cols], in0=ps[4 + q][:, KT + 4 * q:KT + 4 * q + 4], scalar=1.0,
                                         in1=n1w[:, cols], op0=ALU.add, op1=ALU.mult).then_inc(s_redc, 1)
                dve.wait_ge(s_redc, q + 1)
                st.wait()

            def h_tiles(n, src, scale, shift, ready=None):
                for k in range(KT + 1):
                    if n == 0 and k < KT and k % 4 == 0:
                        first_columns(k // 4)
                    if k < KT:
                        if ready:
                            dve.wait_ge(s_xT, ready(k))
                        if k >= 2:
                            dve.wait_ge(s_h, n * KT + k - 1)
                        dve.tensor_scalar(htmp[:, k % 2], src(k), scale[:, k:k + 1], shift[:, k:k + 1],
                                          ALU.mult, ALU.add).then_inc(s_ht, 1)
                    if k >= 1:
                        dve.wait_ge(s_hhi, n * KT + k)
                        dve.tensor_tensor(h[:, k - 1, 1, :], htmp[:, (k - 1) % 2], h[:, k - 1, 0, :].bitcast(F32),
                                          ALU.subtract).then_inc(s_h, 1)
                    if n == 0 and k >= 2 and k % 2 == 0 and k // 2 <= AHEAD:
                        j = k // 2 - 1
                        dve.wait_ge(s_hi, j + 1)
                        dve.tensor_tensor(wlo[:, j], wraw[:, j], whi[:, j].bitcast(F32), ALU.subtract).then_inc(s_lo, 1)

            dve.wait_ge(s_xTc, KT // 2)
            h_tiles(0, lambda k: xT[:, k, :], A1, B1)

            def lo_part(unit, slot, ready):
                dve.wait_ge(s_hi, unit)
                dve.wait_ge(s_pe, ready)
                dve.tensor_tensor(wlo[:, slot], wraw[:, slot], whi[:, slot].bitcast(F32), ALU.subtract).then_inc(s_lo, 1)

            def stream(name, acc_of=None, row0=0, tiles_at=0, cols_at=0):
                ph = PH[name]
                n = ph.units
                with dve.Fori(0, ph.groups) as i:
                    pe0 = i * ph.pe_per + ph.pe0
                    for j in range(AHEAD, n + AHEAD):
                        if j == n + AHEAD - 1:
                            for t in range(0, ph.tiles, 2):
                                if ph.kind == "channel":
                                    dve.wait_ge(s_evt, i * 2 + (ph.chan0 // 2 + t // 2 + 1))
                                    dve.tensor_tensor(proj[:, bass.ds(i * 4 + (tiles_at + t), 2), :], bank[:, t:t + 2, 0:SEQ],
                                                      evt[:, t:t + 2], ALU.add).then_inc(s_evac, 2)
                                else:
                                    for b in range(TB):
                                        dve.wait_ge(s_pe, pe0 + (n - 1 + b + 1))
                                        dve.tensor_copy(vtok[:, b, bass.ds(i * UW + cols_at, UW)], ps[2 + b]).then_inc(s_evac, 1)
                        lo_part(i * n + (ph.unit0 + j + 1), j % RING, pe0 + (j - AHEAD))
                        if ph.ada:
                            a = j - AHEAD
                            ada(acc_of, i * 8 + (ph.ada0 + a - 1 + 4), a % RING, i * 32 + ((ph.ada0 - 2 * KT + a) // RING + 1) * 16,
                                i * 4 + (row0 + a // 2), a % 2)

            dve.wait_ge(s_acc, 48)
            stream("hq_hf", acc, 0, HQ)
            dve.wait_ge(s_acc, 64)
            dve.wait_ge(s_red, 9)
            st.do(dve.tensor_copy(B2, ps[7][:, 0:KT]))
            stream("hi", acc, 0, 0, 0)
            stream("hg", acc, 8, HG)
            dve.wait_ge(s_acc, 80)
            dve.wait_ge(s_red, 10)
            dve.scalar_tensor_tensor(out=A2, in0=ps[7][:, KT:2 * KT], scalar=1.0, in1=n2w, op0=ALU.add,
                                     op1=ALU.mult).then_inc(s_redc, 1)
            dve.wait_ge(s_redc, 5)
            dve.wait_ge(s_v, st.n)
            stream("aq_ak", acc, 0, AQ)
            stream("av", None, 0, 0, HEADS * DH)
            dve.wait_ge(s_gates, 3)
            dve.wait_ge(s_lvm, 1)
            fv, qv = proj[:, HF:HF + 8, :], proj[:, HQ:HQ + 8, :]
            st.then(dve.tensor_tensor(fv, fv, one_lb.unsqueeze(2).to_broadcast([P, 8, SEQ]), ALU.mult))
            st.then(dve.tensor_tensor(fv, fv, lb.unsqueeze(2).to_broadcast([P, 8, SEQ]), ALU.add))
            dve.tensor_scalar(qv, qv, SCALE, None, ALU.mult).then_inc(s_f, 1)
            dve.wait_ge(s_f, 1)
            with dve.Fori(0, HEADS) as hd:
                st.enter(hd, 38)
                f_h = proj[:, bass.ds(hd + HF, 1), :].rearrange("p a t -> p (a t)")
                q_h = proj[:, bass.ds(hd + HQ, 1), :].rearrange("p a t -> p (a t)")
                g_h = proj[:, bass.ds(hd + HG, 1), :].rearrange("p a t -> p (a t)")
                dve.wait_ge(s_cross, hd + 1)
                dve.wait_ge(s_hdone, hd + 1)
                st.do(dve.tensor_scalar(ks[:, 0], f_h, -1.0, 1.0, ALU.mult, ALU.add))
                st.then(dve.tensor_tensor(qp[:, 0], q_h, f_h, ALU.mult))
                seg = f_h
                lv_sems = {3: s_lvA, 7: s_lvB}
                off = 0
                for l in range(LEVELS - 1):
                    w = 1 << l
                    n = SEQ // (2 * w)

                    def halves(a):
                        return a.rearrange("p (n two w) -> p n two w", two=2, w=w)

                    segs = seg.rearrange("p (n two) -> p n two", two=2)
                    first, second = segs[:, :, 0:1], segs[:, :, 1:2]
                    ql, qn, kl, kn = halves(qp[:, l]), halves(qp[:, l + 1]), halves(ks[:, l]), halves(ks[:, l + 1])
                    st.do(dve.tensor_copy(qn[:, :, 0], ql[:, :, 0]))
                    st.do(dve.tensor_copy(kn[:, :, 1], kl[:, :, 1]))
                    st.do(dve.tensor_tensor(qn[:, :, 1], ql[:, :, 1], first.to_broadcast([P, n, w]), ALU.mult))
                    if l < LEVELS - 2:
                        nxt = tot[:, off:off + n]
                        st.do(dve.tensor_tensor(nxt.unsqueeze(2), first, second, ALU.mult))
                        off += n
                        seg = nxt
                    ins = dve.tensor_tensor(kn[:, :, 0], kl[:, :, 0], second.to_broadcast([P, n, w]), ALU.mult)
                    if l == 1:
                        ins.then_inc(s_lvA, 1)
                        dve.wait_ge(s_lvA, hd + 1)
                        st.wait()
                    elif l == 5:
                        ins.then_inc(s_lvB, 1)
                        dve.wait_ge(s_lvB, hd + 1)
                        st.wait()
                    elif l == 6:
                        ins.then_inc(s_lvC, 1)
                    else:
                        st.then(ins)
                dve.wait_ge(s_scA, hd + 1)
                dve.wait_ge(s_scB, hd + 1)
                for b in range(TB):
                    for part, freed in ((0, s_mA), (1, s_mB)):
                        lv = slice(4 * part, 4 * part + 4)
                        ins = dve.tensor_tensor(msk[:, lv, :], ps[4 + 2 * part + b][:, :].rearrange("p (l t) -> p l t", l=4),
                                                lvm[:, lv, :], ALU.mult)
                        if b:
                            ins.then_inc(freed, 1)
                        else:
                            st.do(ins)
                    if b:
                        dve.wait_ge(s_mA, hd + 1)
                        dve.wait_ge(s_mB, hd + 1)
                    else:
                        st.wait()
                    ins = dve.tensor_reduce(aT[:, 2 * b, :], msk[:].rearrange("p l t -> p t l"), AX.X, ALU.add)
                    if b:
                        ins.then_inc(s_aT, 1)
                    else:
                        st.then(ins)
                dve.wait_ge(s_orstd, hd + 1)
                st.then(dve.reciprocal(osq[:], orstd[:]))
                st.then(dve.tensor_tensor(onorm[:], ps[5][:, 0:SEQ], osq[:], ALU.mult))
                dve.scalar_tensor_tensor(out=g_h, in0=onorm[:], scalar=gn, in1=g_h, op0=ALU.mult,
                                         op1=ALU.mult).then_inc(s_hdone, 1)
            st.leave(HEADS)

            dve.wait_ge(s_cs, 2)
            with dve.Fori(0, 8) as j:
                st.enter(j, 2)
                pair = proj[0:ROT, bass.ds(j * 2 + AQ, 2), :]
                dve.wait_ge(s_rotP, j + 1)
                st.do(dve.tensor_tensor(rtmp[0:ROT], ps[7][0:ROT, :].rearrange("p (a t) -> p a t", a=2),
                                        sinr[0:ROT].unsqueeze(1).to_broadcast([ROT, 2, SEQ]), ALU.mult))
                st.do(dve.tensor_tensor(pair, pair, cosr[0:ROT].unsqueeze(1).to_broadcast([ROT, 2, SEQ]), ALU.mult))
                st.wait()
                dve.tensor_tensor(pair, pair, rtmp[0:ROT], ALU.add).then_inc(s_rotU, 1)
                dve.wait_ge(s_rotU, j + 2)
            st.leave(8)
            dve.sem_inc(s_rope, 1)

            with dve.Fori(0, HEADS) as hd:
                st.enter(hd, 6)
                dve.wait_ge(s_S, hd + 1)
                dve.wait_ge(s_pT, hd + 1)
                dve.tensor_tensor(smask[:], ps[4][:, 0:3 * P], neg, ALU.add).then_inc(s_smask, 1)
                dve.wait_ge(s_smask, hd + 2)
                st.do(dve.tensor_reduce(mx[:, 0:1], smask[:, 0:P], AX.X, ALU.max))
                st.then(dve.tensor_reduce(mx[:, 1:2], smask[:, P:], AX.X, ALU.max))
                dve.tensor_scalar(mx, mx, -SCALE, None, ALU.mult).then_inc(s_smax, 1)
                dve.wait_ge(s_prob, hd * 2 + 2)
                st.do(dve.tensor_tensor(prob[:], prob[:], mult, ALU.mult))
                st.wait()
                st.do(dve.tensor_reduce(den[:, 0:1], prob[:, 0:P], AX.X, ALU.add))
                st.then(dve.tensor_reduce(den[:, 1:2], prob[:, P:], AX.X, ALU.add))
                st.then(dve.reciprocal(rden, den))
                dve.tensor_scalar(prob[:, 0:P], prob[:, 0:P], rden[:, 0:1], None, ALU.mult).then_inc(s_pn0, 1)
                dve.tensor_scalar(prob[:, P:], prob[:, P:], rden[:, 1:2], None, ALU.mult).then_inc(s_pn, 1)
            st.leave(HEADS)

            dve.wait_ge(s_mixhi, 1)
            dve.tensor_tensor(h[:, 0:8, 1, :], proj[:, AQ:AQ + 8, :], h[:, 0:8, 0, :].bitcast(F32), ALU.subtract).then_inc(s_mix, 1)
            dve.wait_ge(s_mixhi, 2)
            dve.tensor_tensor(h[:, 8:16, 1, :], proj[:, HG:HG + 8, :], h[:, 8:16, 0, :].bitcast(F32), ALU.subtract).then_inc(s_mix, 1)
            dve.wait_ge(s_mix, 2)
            dve.wait_ge(s_red, 11)
            for q in range(4):
                ins = dve.tensor_copy(g1b[:, q * UW:(q + 1) * UW], ps[4 + q][:, :])
                if q < 3:
                    st.do(ins)
            ins.then_inc(s_redc, 2)
            dve.wait_ge(s_redc, 7)
            st.wait()

            dve.wait_ge(s_xre, 16)
            ph = PH["out"]
            with dve.Fori(0, ph.groups) as i:
                st.enter(i, 2)
                pe0 = i * ph.pe_per + ph.pe0
                for j in range(AHEAD, 8 + AHEAD):
                    lo_part(i * 8 + (ph.unit0 + j + 1), j % RING, pe0 + (j - AHEAD))
                for b in range(TB):
                    cols = bass.ds(i * UW, UW)
                    dve.wait_ge(s_pe, pe0 + (7 + b + 1))
                    st.wait()
                    dve.tensor_tensor(ytmp[:], ps[2 + b][:, :], g1b[:, cols], ALU.mult).then_inc(s_evac, 1)
                    dve.wait_ge(s_evac, i * 2 + (ph.tile0 + b + 1 + 4))
                    st.do(dve.tensor_tensor(x1[:, b, cols], x1[:, b, cols], ytmp[:], ALU.add))
            st.leave(ph.groups)
            st.wait()
            dve.sem_inc(s_ms, 1)
            x_normed(xn, x1, 1).then_inc(s_xn, 1)
            h_tiles(1, lambda k: ps[4 + (k // 2) % 4][:, (k % 2) * SEQ:(k % 2 + 1) * SEQ], A2, B2,
                    lambda k: KT // 2 + k // 2 + 1)

            dve.wait_ge(s_spill, 16)
            dve.wait_ge(s_acc, 96)

            ph = PH["up"]
            chan_groups = ph.chan0 // 4 * 2

            def conv_step(i, half, step):
                dst = up if half else gate

                def w(tap, f):
                    return cw[:, bass.ds(i * 4 + (half * NF + tap * 88 + f), 1)]

                if step == 0:
                    dve.wait_ge(s_evt, i * 2 + (chan_groups + half + 1))
                    dve.tensor_tensor(evt[:], bank[:, 4 * half:4 * half + 4, 0:SEQ], evt[:], ALU.add).then_inc(s_evac, 4)
                elif step == 1:
                    dve.wait_ge(s_evac, i * 8 + (ph.tile0 + 4 * half + 4 + 4))
                    for f in range(4):
                        st.do(dve.tensor_scalar(dst[:, f, :], evt[:, f, :], w(2, f), cb[:, bass.ds(i * 4 + (half * NF + f), 1)],
                                                ALU.mult, ALU.add))
                elif step == 2:
                    st.wait()
                    for f in range(4):
                        st.do(dve.scalar_tensor_tensor(out=dst[:, f, 1:], in0=evt[:, f, :SEQ - 1], scalar=w(1, f),
                                                       in1=dst[:, f, 1:], op0=ALU.mult, op1=ALU.add))
                elif step == 3:
                    st.wait()
                    for f in range(4):
                        ins = dve.scalar_tensor_tensor(out=dst[:, f, 2:], in0=evt[:, f, :SEQ - 2], scalar=w(0, f),
                                                       in1=dst[:, f, 2:], op0=ALU.mult, op1=ALU.add)
                        if f == 3:
                            ins.then_inc(s_convu if half else s_convg, 1)
                        else:
                            st.do(ins)
                elif step == 4 and half:
                    st.wait()
                    dve.wait_ge(s_convu, i + 2)
                    dve.wait_ge(s_silu, i + 1)
                    dve.tensor_tensor(up[:], up[:], gate[:], ALU.mult).then_inc(s_prod, 1)
                elif step == 6 and half:
                    dve.wait_ge(s_acthi, i + 1)
                    dve.wait_ge(s_prod, i + 1)
                    tiles = bass.ds(i * 4, 4)
                    dve.tensor_tensor(act_lo[:, tiles, :], up[:], act_hi[:, tiles, :].bitcast(F32), ALU.subtract).then_inc(s_h, 1)

            def ffn_half(i, half, finished, with_ada):
                pe0 = (i * 2 + half) * ph.pe_per + ph.pe0
                for j in range(AHEAD, 8 + AHEAD):
                    lo_part(i * 16 + (ph.unit0 + half * 8 + j + 1), j % RING, pe0 + (j - AHEAD))
                    if finished:
                        conv_step(i if half else i - 1, 1 - half, j - AHEAD)
                    if with_ada and j % 4 == 1:
                        n = half * 2 + (j - AHEAD) // 4
                        ada(acc_g2, i * 4 + (ph.ada0 + n - 1 + 4), n, i * 16 + ((ph.ada0 - 2 * KT) // RING + 1) * 16,
                            i * 2 + n // 2, n % 2)

            def pair(i, finished, with_ada):
                ffn_half(i, 0, finished, with_ada)
                ffn_half(i, 1, True, with_ada)

            PER = 22
            pair(0, False, True)
            with dve.Fori(1, ph.ada_pairs) as i:
                st.enter(i - 1, PER)
                pair(i, True, True)
            st.leave(ph.ada_pairs - 1)
            with dve.Fori(ph.ada_pairs, ph.groups // 2) as i:
                st.enter(i - ph.ada_pairs, PER)
                pair(i, True, False)
            st.leave(ph.groups // 2 - ph.ada_pairs)

            last = ph.groups // 2 - 1
            ph_down = PH["down"]
            for g in range(ph_down.groups):
                pe0 = ph_down.pe0 + g * ph_down.pe_per
                for j in range(AHEAD, ph_down.units + AHEAD):
                    unit = ph_down.unit0 + g * ph_down.units + j
                    if unit < ph_down.unit0 + ph_down.groups * ph_down.units:
                        lo_part(unit + 1, unit % RING, pe0 + j - AHEAD)
                    if g == 0 and j < AHEAD + 7:
                        conv_step(last, 1, j - AHEAD)
                    if g == 0 and AHEAD + 9 <= j < AHEAD + 13:
                        q = j - AHEAD - 9
                        dve.wait_ge(s_red, 12)
                        ins = dve.tensor_copy(g2b[:, q * UW:(q + 1) * UW], ps[q])
                        if q < 3:
                            st.do(ins)
                        else:
                            ins.then_inc(s_redc, 1)
                if g == 0:
                    dve.wait_ge(s_xr, 32)
                    dve.wait_ge(s_redc, 8)
                for b in range(TB):
                    cols = slice(g * UW, (g + 1) * UW)
                    dve.wait_ge(s_pe, pe0 + ph_down.units - 1 + b + 1)
                    st.wait()
                    dve.tensor_tensor(junk2[:, 0:UW], ps[(4, 6, 0, 2)[g] + b], g2b[:, cols], ALU.mult).then_inc(s_evac, 1)
                    dve.wait_ge(s_evac, ph_down.tile0 + g * 2 + b + 1 + 4)
                    st.do(dve.tensor_tensor(xr[:, b, cols], xr[:, b, cols], junk2[:, 0:UW], ALU.add))
            st.wait()
            dve.sem_inc(s_ms, 1)
            dve.wait_ge(s_rt, 3)
            st.then(dve.reciprocal(ss, rstd))
            for b in range(TB):
                dve.scalar_tensor_tensor(out=xr[:, b, :], in0=xr[:, b, :], scalar=ss[:, b:b + 1], in1=fnb[:],
                                         op0=ALU.mult, op1=ALU.mult).then_inc(s_fin, 1)


_INS = ["x", "c", "positions", "w_ada", "b_ada", "norm1_w", "w_in", "lb_logits", "gnorm_w", "w_out",
        "norm2_w", "w_up", "conv_w", "conv_b", "w_down", "final_norm_w"]


def kernel(**inputs):
    import numpy as _np
    import concourse.bacc as _bacc
    from concourse import mybir as _mybir
    from concourse.bass_utils import run_bass_kernel_spmd as _run

    nc = _bacc.Bacc("TRN2", target_bir_lowering=False, num_devices=1)
    arrays, args = {}, []
    f32, lv = constants()
    for name, a in [(n, _np.ascontiguousarray(inputs[n])) for n in _INS] + [("tab_f32", f32), ("tab_lv", lv)]:
        arrays[f"in_{name}"] = a
        args.append(nc.dram_tensor(f"in_{name}", a.shape, _mybir.dt.from_np(a.dtype), kind="ExternalInput").ap())
    args.append(nc.dram_tensor("out_0", (1, SEQ, D), _mybir.dt.float32, kind="ExternalOutput").ap())
    build(nc, *args)
    r = _run(nc, [arrays], core_ids=[0])
    return r.results[0]["out_0"]
```

```python
from contextlib import ExitStack

import numpy as np

import concourse.bass as bass
from concourse import mybir

F32 = mybir.dt.float32
F32R = mybir.dt.float32r
U8 = mybir.dt.uint8
I32 = mybir.dt.int32
ALU = mybir.AluOpType
ACT = mybir.ActivationFunctionType
AX = mybir.AxisListType

P = 128
SEQ, D, FF = 256, 2048, 5632
KT = D // P
TB = SEQ // P
HEADS, DH = 8, 128
ROT = DH // 4
LEVELS = 8
NF = FF // P
EPS = 1e-6
SCALE = DH ** -0.5
UW = 512
UK = 2
RING = 4
AHEAD = RING
AW = D // 2
HQ, HF, HG, AQ, AK = 0, 8, 16, 24, 32
SH1, SC1, G1, SH2, SC2, G2 = range(6)


class Phase:

    def __init__(self, kind, groups, units, ada, last):
        self.kind, self.groups, self.units, self.ada = kind, groups, units, ada
        self.tiles = 4 if kind == "channel" else 2
        self.unit0, self.tile0, self.pe0, self.ada0, self.chan0 = last
        self.pe_per = units - 1 + self.tiles

    def next(self):
        n = self.groups
        return (self.unit0 + n * self.units, self.tile0 + n * self.tiles, self.pe0 + n * self.pe_per,
                self.ada0 + n * self.ada, self.chan0 + n * self.tiles * (self.kind == "channel"))


def phases():
    at, out = (0, 0, 1, 2 * KT, 0), {}
    for name, kind, groups, units, ada in (
            ("hq_hf", "channel", 4, 8, 8), ("hi", "token", 2, 8, 8), ("hg", "channel", 2, 8, 8),
            ("aq_ak", "channel", 4, 8, 8), ("av", "token", 2, 8, 0), ("out", "token", 4, 8, 0),
            ("up", "channel", 22, 8, 0), ("down", "token", 4, 22, 0)):
        out[name] = Phase(kind, groups, units, ada, at)
        at = out[name].next()
        if name == "up":
            out["up"].ada_pairs = 8
            at = at[:3] + (at[3] + 32,) + at[4:]
    return out


class Group:

    def __init__(self, ph, n):
        self.kind, self.units, self.tiles, self.pe_per, self.ada = ph.kind, ph.units, ph.tiles, ph.pe_per, ph.ada
        self.unit0, self.tile0 = ph.unit0 + n * ph.units, ph.tile0 + n * ph.tiles
        self.pe0, self.ada0, self.chan0 = ph.pe0 + n * ph.pe_per, ph.ada0 + n * ph.ada, ph.chan0 + n * ph.tiles
        self.bank0 = self.tile0 % 8


def slot_free(ph, pe0, j):
    return pe0 + (ph.pe_per if j - RING == ph.units - 1 else j - RING + 1)


class Steps:

    def __init__(self, eng, sem):
        self.eng, self.sem, self.n, self.base = eng, sem, 0, 0

    def do(self, ins):
        ins.then_inc(self.sem, 1)
        self.n += 1

    def wait(self):
        self.eng.wait_ge(self.sem, self.base + self.n)

    def then(self, ins):
        self.do(ins)
        self.wait()

    def enter(self, i, per):
        self.start, self.per, self.base, self.n = self.n, per, self.n + i * per, 0

    def leave(self, times):
        assert self.n == self.per, (self.n, self.per)
        self.base, self.n = 0, self.start + times * self.per


def constants():
    t, s = np.arange(P)[:, None], np.arange(P)[None, :]

    def mult(d):
        return ((d >= 0) & (d <= 128)).astype(int) + ((d >= 0) & (d % 4 == 0)) + ((d >= 0) & (d % 16 == 0))

    m = np.concatenate([mult(t - s), mult(t - s + P), mult(t - s)], 1).astype(np.float32)
    neg = np.where(m > 0, 0, -1e30).astype(np.float32)
    rot = np.zeros((P, P), np.float32)
    for j in range(ROT // 2):
        rot[j + ROT // 2, j], rot[j, j + ROT // 2] = -1, 1
    freq = np.zeros((P, 1), np.float32)
    inv = (1.0 / (np.float32(500000.0) ** (np.arange(0, ROT, 2, dtype=np.float32) / np.float32(ROT)))).astype(np.float32)
    freq[:ROT, 0] = np.concatenate([inv, inv])
    f32 = np.concatenate([np.eye(P, dtype=np.float32), rot, neg, m, freq], 1)
    s, t = np.arange(P)[:, None], np.arange(P)[None, :]
    lv = [(s == t)] + [((s >> (l + 1)) == (t >> (l + 1))) & ((s >> l) % 2 == 0) & ((t >> l) % 2 == 1) for l in range(LEVELS - 1)]
    return f32, np.stack(lv, 1).reshape(P, LEVELS * P).astype(np.float32)


def build(nc, x, c, positions, w_ada, b_ada, norm1_w, w_in, lb_logits, gnorm_w, w_out,
          norm2_w, w_up, conv_w, conv_b, w_down, final_norm_w, tab_f32, tab_lv, out):
    PH = phases()
    w_in, w_out, w_up, w_down, w_ada = (w.rearrange("o k n -> (o k) n") for w in (w_in, w_out, w_up, w_down, w_ada))
    x_tok = x.rearrange("o (b p) d -> p (o b) d", p=P)
    out_tok = out.rearrange("o (b p) d -> p (o b) d", p=P)
    x1_dram = nc.dram_tensor("x1_spill", (P, TB, D), F32, kind="Internal").ap()

    with ExitStack() as ctx:
        def at(off, name, shape, dt=F32):
            return nc.alloc_sbuf_tensor_at(name, [P] + shape, dt, offset=BASE + off)

        def sem(name):
            return ctx.enter_context(nc.semaphore(name))

        BASE = 16512
        K = 1024
        wraw = at(0, "wraw", [RING, UK, UW])
        araw = at(16 * K, "araw", [RING, AW])
        whi = at(32 * K, "whi", [RING, UK, UW], F32R)
        wlo = at(48 * K, "wlo", [RING, UK, UW], F32R)
        astart = at(32 * K, "astart", [RING, D])
        h = at(64 * K, "h", [KT, 2, SEQ], F32R)
        xr = at(64 * K, "xr", [TB, D])
        g2b = at(80 * K, "g2b", [D])
        fnb = at(88 * K, "fnb", [D])
        Z = 96 * K
        proj = at(Z, "proj", [40, SEQ])
        x0 = at(Z, "x0", [TB, D])
        xT = at(Z + 16 * K, "xT", [KT, SEQ])
        acc_b = at(Z + 32 * K, "acc_b", [D])
        x1 = at(Z, "x1", [TB, D])
        g1b = at(Z + 56 * K, "g1b", [D])
        xn = at(Z + 24 * K, "xn", [TB, D])
        vtok = at(Z + 40 * K, "vtok", [TB, 2 * HEADS * DH])
        rows = at(Z + 40 * K, "rows", [6, P])
        qp = at(Z + 56 * K, "qp", [LEVELS, SEQ])
        ks = at(Z + 64 * K, "ks", [LEVELS, SEQ])
        rtmp8 = at(Z + 56 * K, "rtmp8", [8, SEQ])
        junk = at(Z + 56 * K, "junk", [D])
        htmp = at(Z + 64 * K, "htmp", [2, SEQ])
        ytmp = at(Z + 66 * K, "ytmp", [UW])
        tot = at(Z + 72 * K, "tot", [SEQ])
        aT = at(Z + 73 * K, "aT", [P])
        hv = at(Z + 75 * K, "hv", [TB, DH])
        osq = at(Z + 76 * K, "osq", [SEQ])
        aq = at(Z + 79 * K, "aq", [SEQ])
        avh = at(Z + 80 * K, "avh", [TB, DH])
        smask = at(Z + 81 * K, "smask", [3 * P])
        lvl = at(Z + 81 * K, "lvl", [LEVELS, P])
        acc_c = at(Z + 72 * K, "acc_c", [D])
        msk = at(64 * K, "msk", [TB, LEVELS, P])

        prob = at(Z + 83 * K, "prob", [3 * P])
        probT = at(Z + 85 * K, "probT", [3 * P])
        cosr = at(Z + 87 * K, "cosr", [SEQ])
        sinr = at(Z + 88 * K, "sinr", [SEQ])
        rtmp = at(Z + 89 * K, "rtmp", [2, SEQ])
        acc = at(Z + 91 * K, "acc", [D])
        tab = at(Z + 99 * K, "tab", [7 * P + 1])
        lvm = at(Z + 103 * K, "lvm", [LEVELS, P], U8)
        act_hi = at(Z, "act_hi", [NF, SEQ], F32R)
        act_lo = at(Z + 44 * K, "act_lo", [NF, SEQ], F32R)
        gate = at(Z + 88 * K, "gate", [4, SEQ])
        up = at(Z + 92 * K, "up", [4, SEQ])
        acc_g2 = at(Z + 96 * K, "acc_g2", [D])
        junk2 = at(Z + 88 * K, "junk2", [D])
        Q = Z + 104 * K
        ident = at(Q, "ident", [P])
        ones = at(Q + 512, "ones", [P])
        evt = at(Z + 111 * K + 864 - 4 * K, "evt", [4, SEQ])
        NPRM = 65 + 4 * 88
        prm = at(Q + K, "prm", [NPRM])
        small = at(Q + K + 4 * NPRM + 28, "small", [192])
        assert Q + K + 4 * NPRM + 28 + 192 * 4 <= Z + 107 * K + 864 and BASE + Z + 111 * K + 864 <= 229368
        rot, neg, mult, freq = tab[:, 0:P], tab[:, P:4 * P], tab[:, 4 * P:7 * P], tab[:, 7 * P:7 * P + 1]
        n1w, n2w, lbl = prm[:, 16:32], prm[:, 32:48], prm[:, 48:64]
        gn = prm[:, 64:65]
        cw, cb = prm[:, 65:65 + 264], prm[:, 65 + 264:65 + 352]
        csilu = small[:, 0:16]
        A1, B1, A2, B2 = (small[:, 16 + 16 * j:32 + 16 * j] for j in range(4))
        lb, one_lb, lbm = small[:, 80:88], small[:, 88:96], small[:, 96:104]
        lbe = small[:, 104:120]
        ss, rstd = small[:, 120:122], small[:, 122:124]
        mx, den = small[:, 124:126], small[:, 126:128]
        rden = small[:, 128:130]
        epsc = small[:, 130:131]

        bank = ctx.enter_context(nc.psum_tensor("bank", [P, 8, 512], F32))
        ps = [bank[:, b, :] for b in range(8)]

        s_in = sem("s_in")
        s_inc = sem("s_inc")
        s_cst = sem("s_cst")
        s_lvm = sem("s_lvm")
        s_x = sem("s_x")
        s_xre = sem("s_xre")
        s_w = [sem(f"s_w{j}") for j in range(RING)]
        s_as = [sem(f"s_as{j}") for j in range(RING)]
        s_a = [sem(f"s_a{j}") for j in range(RING)]
        s_hi = sem("s_hi")
        s_lo = sem("s_lo")
        s_ada = sem("s_ada")
        s_pe = sem("s_pe")
        s_evt = sem("s_evt")
        s_evac = sem("s_evac")
        s_acc = sem("s_acc")
        s_acc_c = sem("s_acc_c")
        s_red = sem("s_red")
        s_redc = sem("s_redc")
        s_v = sem("s_v")
        s_s = sem("s_s")
        s_p = sem("s_p")
        s_prmT = sem("s_prmT")
        s_prm = sem("s_prm")
        s_csilu = sem("s_csilu")
        s_lbd = sem("s_lbd")
        s_lbe = sem("s_lbe")
        s_ms = sem("s_ms")
        s_rt = sem("s_rt")
        s_xn = sem("s_xn")
        s_xT = sem("s_xT")
        s_xTc = sem("s_xTc")
        s_ht = sem("s_ht")
        s_hhi = sem("s_hhi")
        s_h = sem("s_h")
        s_ang = sem("s_ang")
        s_cs = sem("s_cs")
        s_gates = sem("s_gates")
        s_f = sem("s_f")
        s_rotP = sem("s_rotP")
        s_rotU = sem("s_rotU")
        s_rope = sem("s_rope")
        s_rope0 = sem("s_rope0")
        s_hv = sem("s_hv")
        s_lvA = sem("s_lvA")
        s_lvB = sem("s_lvB")
        s_lvC = sem("s_lvC")
        s_scA = sem("s_scA")
        s_scB = sem("s_scB")
        s_mA = sem("s_mA")
        s_m0 = sem("s_m0")
        s_mB = sem("s_mB")
        s_cross = sem("s_cross")
        s_crossC = sem("s_crossC")
        s_oT = sem("s_oT")
        s_osq = sem("s_osq")
        s_oss = sem("s_oss")
        s_orstd = sem("s_orstd")
        s_oc = sem("s_oc")
        s_hdone = sem("s_hdone")
        s_aq = sem("s_aq")
        s_avh = sem("s_avh")
        s_S = sem("s_S")
        s_smask = sem("s_smask")
        s_smax = sem("s_smax")
        s_prob = sem("s_prob")
        s_pn = sem("s_pn")
        s_pT = sem("s_pT")
        s_pTc = sem("s_pTc")
        s_ao = sem("s_ao")
        s_aoc = sem("s_aoc")
        s_mixhi = sem("s_mixhi")
        s_mix = sem("s_mix")
        s_spill = sem("s_spill")
        s_silu = sem("s_silu")
        s_convg = sem("s_convg")
        s_convu = sem("s_convu")
        s_acthi = sem("s_acthi")
        s_xr = sem("s_xr")
        s_prod = sem("s_prod")
        s_pn0 = sem("s_pn0")
        s_fin = sem("s_fin")
        s_out = sem("s_out")

        block = ctx.enter_context(nc.Block())

        @block.sync
        def _(sp):
            def load_unit(w, unit, slot, k0, col):
                sp.wait_ge(s_lo, unit + 1)
                src = w[k0:k0 + UK * P, bass.ds(col, UW)].rearrange("(k p) n -> p k n", p=P)
                sp.dma_start(wraw[:, slot], src).then_inc(s_w[slot], 16)

            def load_ada(number, slot, mod, row, half):
                sp.wait_ge(s_ada, number + 1)
                src = w_ada[bass.ds(row, P), mod * D + half * AW:mod * D + (half + 1) * AW]
                sp.dma_start(araw[:, slot], src).then_inc(s_a[slot], 16)

            with sp.Fori(0, KT // 2) as r:
                for n, (mod, row) in enumerate(((SH1, 0), (SC1, 0), (SH1, 1), (SC1, 1))):
                    sp.wait_ge(s_ada, r * 4 + (n + 1))
                    sp.dma_start(astart[:, n], w_ada[bass.ds(r * (2 * P) + row * P, P), mod * D:(mod + 1) * D]).then_inc(s_as[n], 16)

            def phase(name, w, col0, mod=None, row0=0, before=None):
                ph = PH[name]

                def group(i):
                    for j in range(ph.units):
                        load_unit(w, i * ph.units + (ph.unit0 + j), j % RING, j * UK * P, i * UW + col0)
                        a, m, row = j - AHEAD, mod, row0
                        if a < 0 and isinstance(i, int) and i == 0:
                            m, row = before or (None, None)
                        if m is not None:
                            load_ada(i * 8 + (ph.ada0 + a), a % RING, m, i * (4 * P) + (row + a // 2) * P, a % 2)

                group(0)
                if ph.groups == 2:
                    group(1)
                else:
                    with sp.Fori(1, ph.groups) as i:
                        group(i)

            phase("hq_hf", w_in, 3072, SH2)
            phase("hi", w_in, 5120, SC2, 0, (SH2, KT))
            phase("hg", w_in, 6144, SC2, 8, (SC2, 8))
            phase("aq_ak", w_in, 0, G1, 0, (SC2, KT))
            phase("av", w_in, 2048, None, 0, (G1, KT))
            phase("out", w_out, 0)

            ph = PH["up"]

            def pairs(first, last, ada):
                with sp.Fori(first, last) as i:
                    for half in range(2):
                        for j in range(8):
                            load_unit(w_up, i * 16 + (ph.unit0 + half * 8 + j), j % RING, j * UK * P, i * UW + half * FF)
                            if ada and j % 4 == 1:
                                n = half * 2 + j // 4
                                load_ada(i * 4 + (ph.ada0 + n), n, G2, i * (2 * P) + n // 2 * P, n % 2)

            pairs(0, ph.ada_pairs, True)
            pairs(ph.ada_pairs, ph.groups // 2, False)
            ph = PH["down"]
            with sp.Fori(0, ph.groups // 2) as i:
                for half in range(2):
                    for j in range(ph.units):
                        n = half * ph.units + j
                        load_unit(w_down, i * (2 * ph.units) + (ph.unit0 + n), n % RING, j * UK * P, i * (2 * UW) + half * UW)
            for b in range(TB):
                for part in range(2):
                    cols = slice(part * AW, (part + 1) * AW)
                    sp.wait_ge(s_fin, 2 * b + part + 1)
                    sp.dma_start(out_tok[:, b, cols], xr[:, b, cols]).then_inc(s_out, 16)
            sp.wait_ge(s_out, 4 * 16)

        @block.gpsimd
        def _(gp):
            st = Steps(gp, s_p)
            gp.memset(ones[:], 1.0).then_inc(s_cst, 1)
            gp.memset(epsc, EPS).then_inc(s_cst, 1)
            def init_acc(a, mod, done=s_acc):
                st.then(gp.memset(a[:], 0.0))
                gp.dma_start(a[0:1, :], b_ada[:, mod * D:(mod + 1) * D]).then_inc(done, 16)

            init_acc(acc, SH1)
            init_acc(acc_b, SC1)
            for t in range(3):
                gp.dma_start(rows[0:88, 1 + t, :], conv_w[0, t].rearrange("(r p) -> r p", p=P)).then_inc(s_in, 16)
            gp.dma_start(rows[0:88, 4, :], conv_b.rearrange("o (r p) -> (o r) p", p=P)).then_inc(s_in, 16)
            gp.dma_start(tab[:], tab_f32[:, P:]).then_inc(s_in, 16)
            gp.dma_start(lvl[:].rearrange("p l t -> p (l t)"), tab_lv).then_inc(s_in, 16)
            gp.dma_start(rtmp[0:ROT, 0, :].bitcast(I32), positions.to_broadcast([ROT, SEQ])).then_inc(s_in, 16)

            gp.wait_ge(s_in, 7 * 16)
            gp.tensor_copy(lvm[:], lvl[:]).then_inc(s_lvm, 1)

            gp.wait_ge(s_red, 8)
            init_acc(acc, SH2)
            init_acc(acc_c, SC2, s_acc_c)
            gp.wait_ge(s_red, 9)
            init_acc(acc, G1)
            gp.wait_ge(s_evac, PH["out"].tile0 + 4)
            gp.wait_ge(s_red, 10)
            gp.wait_ge(s_rope, 1)
            with gp.Fori(0, HEADS) as hd:
                gp.wait_ge(s_smask, hd + 1)
                gp.tensor_copy(aq[:], proj[:, bass.ds(hd + AQ, 1), :].rearrange("p a t -> p (a t)")).then_inc(s_aq, 1)
                gp.wait_ge(s_oT, hd + 1)
                gp.tensor_copy(hv[:], vtok[:, :, bass.ds(hd * DH, DH)]).then_inc(s_hv, 1)
                gp.wait_ge(s_ao, hd + 1)
                gp.tensor_copy(avh[:], vtok[:, :, bass.ds(hd * DH + HEADS * DH, DH)]).then_inc(s_avh, 1)
            gp.wait_ge(s_mix, 3)
            gp.dma_start(x1[:], x_tok).then_inc(s_xre, 16)
            gp.wait_ge(s_red, 11)
            init_acc(acc_g2, G2)
            gp.wait_ge(s_h, 2 * KT)
            gp.dma_start(x1_dram, x1[:]).then_inc(s_spill, 16)
            gp.wait_ge(s_spill, 16)
            gp.wait_ge(s_pe, PH["down"].pe0)
            gp.dma_start(xr[:], x1_dram).then_inc(s_xr, 16)
            gp.dma_start(fnb[:], final_norm_w.rearrange("(o d) -> o d", o=1).to_broadcast([P, D])).then_inc(s_xr, 16)

        @block.scalar
        def _(act):
            st = Steps(act, s_s)
            for start in (s_aoc, s_orstd):
                act.sem_inc(start, 1)

            r0 = 0
            for src in (c.rearrange("o (r p) -> (o r) p", p=P), norm1_w.rearrange("o (r p) -> (o r) p", p=P),
                        norm2_w.rearrange("o (r p) -> (o r) p", p=P), lb_logits.rearrange("o (r p) -> (o r) p", p=P),
                        gnorm_w):
                n = src.shape[0]
                act.dma_start(rows[r0:r0 + n, 0, :], src).then_inc(s_inc, 16)
                r0 += n
            act.dma_start(ident[:], tab_f32[:, 0:P]).then_inc(s_inc, 16)
            act.dma_start(x0[:], x_tok).then_inc(s_x, 16)

            def hi_part(slot, count, ready=None):
                act.wait_ge(s_w[slot], count)
                if ready is not None:
                    act.wait_ge(s_pe, ready)
                act.activation(whi[:, slot], wraw[:, slot], ACT.Copy).then_inc(s_hi, 1)

            def hi_ahead(ph, unit0, i, j, pe0, loads):
                hi_part((unit0 + j) % RING, i * loads + ((unit0 + j) // RING + 1) * 16, slot_free(ph, pe0, j))

            def lo_columns(pair, bank0):
                b = bank0 + 2 * pair
                act.activation(evt[:, 2 * pair:2 * pair + 2], bank[:, b:b + 2, 256:512], ACT.Copy).then_inc(s_evt, 1)

            def stream(name):
                with act.Fori(0, PH[name].groups // 2) as turn:
                    i = turn * 2
                    for ph in (PH[name], Group(PH[name], 1)):
                        pe0 = i * ph.pe_per + ph.pe0
                        n = ph.units
                        for j in range(AHEAD, n + AHEAD):
                            if j == n + AHEAD - 1 and ph.kind == "channel":
                                for pair in range(2):
                                    act.wait_ge(s_pe, pe0 + (n - 1 + 2 * pair + 2))
                                    act.wait_ge(s_evac, i * 4 + (ph.tile0 + 2 * pair - 2 + 4))
                                    lo_columns(pair, ph.tile0 % 8)
                            hi_ahead(ph, ph.unit0, i, j, pe0, n // RING * 16)

            act.wait_ge(s_prm, 1)
            act.activation(csilu, prm[:, 0:16], ACT.Silu).then_inc(s_csilu, 1)
            act.wait_ge(s_lbd, 1)
            act.activation(lbe, lbe, ACT.Exp).then_inc(s_lbe, 1)

            def norm_sums(src, squares):
                for b in range(TB):
                    if b:
                        st.wait()
                    st.do(act.activation(squares[:], src[:, b, :], ACT.Square, accum_out=ss[:, b:b + 1]))
                st.wait()
                act.activation(rstd, ss, ACT.Sqrt, bias=epsc, scale=1.0 / D).then_inc(s_rt, 1)

            act.wait_ge(s_x, 16)
            act.wait_ge(s_cst, 2)
            norm_sums(x0, junk)
            for k in range(KT // 2):
                act.wait_ge(s_xT, k + 1)
                act.activation(xT[:, 2 * k:2 * k + 2, :], ps[4 + k % 4][:, :].rearrange("p (a t) -> p a t", a=2),
                               ACT.Copy).then_inc(s_xTc, 1)
            act.wait_ge(s_ang, 1)
            act.activation(sinr[0:ROT], sinr[0:ROT], ACT.Sin).then_inc(s_cs, 1)
            act.activation(cosr[0:ROT], cosr[0:ROT], ACT.Sin).then_inc(s_cs, 1)
            def h_hi(n):
                for k in range(KT):
                    act.wait_ge(s_ht, n * KT + k + 1)
                    act.activation(h[:, k, 0, :], htmp[:, k % 2], ACT.Copy).then_inc(s_hhi, 1)
                    if n == 0 and k % 2 and k // 2 < AHEAD:
                        act.wait_ge(s_ada, 2 * KT + 4)
                        hi_part(k // 2, 16)

            h_hi(0)
            stream("hq_hf")
            stream("hi")
            act.wait_ge(s_evac, PH["hi"].tile0 + 4)
            act.activation(proj[:, HQ:HQ + 8, :], proj[:, HQ:HQ + 8, :], ACT.Silu).then_inc(s_gates, 1)
            stream("hg")
            act.activation(proj[:, HF:HF + 8, :], proj[:, HF:HF + 8, :], ACT.Sigmoid).then_inc(s_gates, 1)
            stream("aq_ak")
            act.wait_ge(s_evac, PH["aq_ak"].tile0 + 4)
            act.activation(proj[:, HG:HG + 8, :], proj[:, HG:HG + 8, :], ACT.Silu).then_inc(s_gates, 1)
            stream("av")
            with act.Fori(0, HEADS) as hd:
                act.wait_ge(s_smax, hd + 1)
                act.activation(prob[:, 0:P], smask[:, 0:P], ACT.Exp, bias=mx[:, 0:1], scale=SCALE).then_inc(s_prob, 1)
                act.activation(prob[:, P:], smask[:, P:], ACT.Exp, bias=mx[:, 1:2], scale=SCALE).then_inc(s_prob, 1)
                act.wait_ge(s_cross, hd + 2)
                act.activation(aT[:], ps[4][:, 0:P], ACT.Copy).then_inc(s_crossC, 1)
                act.wait_ge(s_oT, hd + 2)
                act.activation(proj[:, bass.ds(hd + HQ, 1), :].rearrange("p a t -> p (a t)"), ps[3][:, 0:SEQ],
                               ACT.Copy).then_inc(s_oc, 1)
                act.activation(osq[:], ps[3][:, 0:SEQ], ACT.Square).then_inc(s_osq, 1)
                act.wait_ge(s_pT, hd + 2)
                act.activation(probT[:], ps[1][:, 0:3 * P], ACT.Copy).then_inc(s_pTc, 1)
                act.wait_ge(s_oss, hd + 1)
                act.activation(proj[:, bass.ds(hd + HF, 1), :].rearrange("p a t -> p (a t)"), ps[3][:, SEQ:2 * SEQ],
                               ACT.Sqrt, bias=epsc, scale=1.0 / DH).then_inc(s_orstd, 1)
                act.wait_ge(s_ao, hd + 2)
                act.activation(proj[:, bass.ds(hd + AQ, 1), :].rearrange("p a t -> p (a t)"), ps[2][:, 0:SEQ],
                               ACT.Copy).then_inc(s_aoc, 1)
            act.wait_ge(s_aoc, HEADS + 1)
            act.activation(h[:, 0:8, 0, :], proj[:, AQ:AQ + 8, :], ACT.Copy).then_inc(s_mixhi, 1)
            for half in range(2):
                act.wait_ge(s_hdone, half + 1)
                act.activation(h[:, 8 + 4 * half:12 + 4 * half, 0, :], proj[:, HG + 4 * half:HG + 4 * half + 4, :],
                               ACT.Copy).then_inc(s_mixhi, 1)
            stream("out")

            act.wait_ge(s_evac, PH["up"].tile0 + 4)
            act.wait_ge(s_ms, 1)
            norm_sums(x1, junk)
            h_hi(1)

            ph = PH["up"]

            def ffn_half(i, half, finished):
                pe0 = (i * 2 + half) * ph.pe_per + ph.pe0
                banks = bank[:, 4 - 4 * half:8 - 4 * half, 256:512]
                for j in range(AHEAD, 8 + AHEAD):
                    hi_ahead(ph, ph.unit0 + half * 8, i, j, pe0, 64)
                    if j == AHEAD and finished:
                        if half:
                            act.wait_ge(s_convu, i + 1)
                        else:
                            act.wait_ge(s_convg, i)
                        act.activation(evt[:], banks, ACT.Copy).then_inc(s_evt, 1)
                    if j == AHEAD + 5:
                        if half:
                            act.wait_ge(s_convg, i + 1)
                            act.activation(gate[:], gate[:], ACT.Silu).then_inc(s_silu, 1)
                        elif finished:
                            act.wait_ge(s_prod, i)
                            act.activation(act_hi[:, bass.ds(i * 4 - 4, 4), :], up[:], ACT.Copy).then_inc(s_acthi, 1)

            ffn_half(0, 0, False)
            ffn_half(0, 1, True)
            with act.Fori(1, ph.groups // 2) as i:
                ffn_half(i, 0, True)
                ffn_half(i, 1, True)
            ph = PH["down"]
            for g in range(ph.groups):
                for j in range(AHEAD, ph.units + AHEAD):
                    if g == 0 and j == AHEAD:
                        act.wait_ge(s_convg, 11)
                        act.activation(evt[:], bank[:, 4:8, 256:512], ACT.Copy).then_inc(s_evt, 1)
                    unit = ph.unit0 + g * ph.units + j
                    if unit < ph.unit0 + ph.groups * ph.units:
                        hi_part(unit % RING, (unit // RING + 1) * 16, slot_free(ph, ph.pe0 + g * ph.pe_per, j))
                    if g == 0 and j == AHEAD + 5:
                        act.wait_ge(s_prod, 11)
                        act.activation(act_hi[:, NF - 4:, :], up[:], ACT.Copy).then_inc(s_acthi, 1)
            act.wait_ge(s_ms, 2)
            norm_sums(xr, junk2)

        @block.tensor
        def _(pe):
            for start in (s_pe, s_oT, s_cross, s_ao, s_pT):
                pe.sem_inc(start, 1)
            pe.wait_ge(s_inc, 6 * 16)
            pe.transpose(ps[0][:, 0:65], rows[0:65, 0, :], ident[0:65, 0:65]).then_inc(s_prmT, 1)
            pe.wait_ge(s_in, 7 * 16)
            pe.wait_ge(s_prm, 1)
            for t in range(4):
                last = pe.transpose(ps[0][:, 65 + 88 * t:65 + 88 * (t + 1)], rows[0:88, 1 + t, :], ident[0:88, 0:88])
            last.then_inc(s_prmT, 1)

            def x_transposes(src, n, k0=0, k1=KT // 2):
                for k in range(k0, k1):
                    if k >= 4:
                        if n == 0:
                            pe.wait_ge(s_xTc, k - 3)
                        else:
                            pe.wait_ge(s_ht, KT + 2 * (k - 3))
                    for a in range(2):
                        for b in range(TB):
                            last = pe.transpose(ps[4 + k % 4][:, a * SEQ + b * P:a * SEQ + (b + 1) * P],
                                                src[:, b, (2 * k + a) * P:(2 * k + a + 1) * P], ident[:])
                    last.then_inc(s_xT, 1)

            pe.wait_ge(s_xn, 1)
            x_transposes(x0, 0)

            def mod_columns(a, col, k0=0, k1=KT, bank0=7):
                for k in range(k0, k1):
                    last = pe.matmul(ps[bank0][:, col + k:col + k + 1], a[:, k * P:(k + 1) * P], ones[:, 0:1],
                                     start=True, stop=True)
                last.then_inc(s_red, 1)

            def channel_group(ph, i, h_done, bank0=0, reuse=4, between=None):
                for j in range(ph.units):
                    slot = (ph.unit0 + j) % RING
                    pe.wait_ge(s_lo, i * ph.units + (ph.unit0 + j + 1 + 4))
                    pe.wait_ge(s_h, h_done + UK * (j + 1))
                    for f in range(4):
                        out = ps[bank0 + f]
                        if j == 0 and (ph.tile0 >= 8 or not isinstance(i, int)):
                            pe.wait_ge(s_evac, i * 4 + (ph.tile0 + f - reuse + 1 + 4))
                        cols = slice(f * P, (f + 1) * P)
                        for k in range(UK):
                            kk = j * UK + k
                            pe.matmul(out, whi[:, slot, k, cols], h[:, kk].rearrange("p a t -> p (a t)"),
                                      start=(kk == 0), stop=False, skip_group_check=True)
                            last = pe.matmul(out[:, 0:SEQ], wlo[:, slot, k, cols], h[:, kk, 0, :],
                                             start=False, stop=(kk == KT - 1), skip_group_check=True)
                        if j == ph.units - 1:
                            last.then_inc(s_pe, 1)
                    if j < ph.units - 1:
                        last.then_inc(s_pe, 1)
                    if between:
                        between(j)

            def token_group(ph, i, hi, lo, unit0=None, bank0=2, reuse=2, ready=None, ready_sem=s_h):
                for j in range(ph.units):
                    slot = (ph.unit0 + j) % RING if unit0 is None else (unit0 + j) % RING
                    pe.wait_ge(s_lo, i * ph.units + (ph.unit0 + j + 1 + 4))
                    if ready:
                        pe.wait_ge(ready_sem, ready(j))
                    for b in range(TB):
                        if j == 0:
                            pe.wait_ge(s_evac, i * 2 + (ph.tile0 + b - reuse + 1 + 4))
                        for k in range(UK):
                            kk = j * UK + k
                            first, end = kk == 0, kk == ph.units * UK - 1
                            pe.matmul(ps[bank0 + b], hi(kk, b), whi[:, slot, k, :], start=first, stop=False)
                            pe.matmul(ps[bank0 + b], hi(kk, b), wlo[:, slot, k, :], start=False, stop=False)
                            last = pe.matmul(ps[bank0 + b], lo(kk, b), whi[:, slot, k, :], start=False, stop=end)
                        if j == ph.units - 1:
                            last.then_inc(s_pe, 1)
                    if j < ph.units - 1:
                        last.then_inc(s_pe, 1)

            def h_hi(k, b):
                return h[:, k, 0, b * P:(b + 1) * P]

            def h_lo(k, b):
                return h[:, k, 1, b * P:(b + 1) * P]

            pe.wait_ge(s_ada, 2 * KT + 4)
            pe.wait_ge(s_xTc, KT // 2)
            pe.wait_ge(s_prm, 2)

            def first_columns(q):
                mod_columns(acc, 0, 4 * q, 4 * q + 4, 4 + q)
                mod_columns(acc_b, KT, 4 * q, 4 * q + 4, 4 + q)

            first_columns(0)
            first_columns(1)
            def groups(name, first=0):
                with pe.Fori(first, PH[name].groups // 2) as turn:
                    for ph in (PH[name], Group(PH[name], 1)):
                        channel_group(ph, turn * 2, 0, ph.tile0 % 8, 8)

            channel_group(PH["hq_hf"], 0, 0, 0, 8, between=lambda j: first_columns(2 + j // 2) if j in (0, 2) else None)
            pe.wait_ge(s_redc, 4)
            channel_group(Group(PH["hq_hf"], 1), 0, 0, 4, 8)
            groups("hq_hf", 1)
            token_group(PH["hi"], 0, h_hi, h_lo, bank0=0, reuse=8)
            pe.wait_ge(s_ada, PH["hi"].ada0 + 4)
            pe.wait_ge(s_evac, PH["hi"].tile0 + 4)
            mod_columns(acc, 0)
            token_group(Group(PH["hi"], 1), 0, h_hi, h_lo, bank0=2, reuse=8)
            pe.wait_ge(s_redc, 5)
            groups("hg")
            groups("aq_ak")
            token_group(PH["av"], 0, h_hi, h_lo, bank0=4, reuse=8)

            def rotated(part):
                for b in range(4):
                    a = (AQ, AK)[part] + 2 * b
                    last = pe.matmul(ps[b], rot, proj[:, a:a + 2, :].rearrange("p a t -> p (a t)"), start=True, stop=True)
                last.then_inc(s_rotP, 1)

            pe.wait_ge(s_evac, PH["av"].tile0 + 4)
            rotated(0)
            token_group(Group(PH["av"], 1), 0, h_hi, h_lo, bank0=6, reuse=8)
            pe.wait_ge(s_ada, PH["aq_ak"].ada0 + 4)
            pe.wait_ge(s_evac, PH["av"].tile0 + 2 + 4)
            mod_columns(acc_c, KT, bank0=4)
            pe.wait_ge(s_rotU, 2)
            rotated(1)

            pe.wait_ge(s_f, 1)
            pe.wait_ge(s_redc, 6)
            pe.wait_ge(s_rope, 1)
            with pe.Fori(0, HEADS) as hd:
                q_h = proj[:, bass.ds(hd + HQ, 1), :].rearrange("p a t -> p (a t)")
                k_h = proj[:, bass.ds(hd + AK, 1), :].rearrange("p a t -> p (a t)")
                pe.wait_ge(s_aq, hd + 1)
                pe.wait_ge(s_smask, hd + 1)
                pe.matmul(ps[0][:, 0:P], aq[:, 0:P], k_h[:, 0:P], start=True, stop=True)
                pe.matmul(ps[0][:, P:3 * P], aq[:, P:SEQ], k_h, start=True, stop=True).then_inc(s_S, 1)
                pe.wait_ge(s_lvA, hd + 1)
                for b in range(TB):
                    tok = slice(b * P, (b + 1) * P)
                    pe.matmul(ps[4 + b][:, 0:P], ks[:, 0, tok], q_h[:, tok], start=True, stop=True)
                    for l in range(3):
                        last = pe.matmul(ps[4 + b][:, (l + 1) * P:(l + 2) * P], ks[:, l, tok], qp[:, l, tok],
                                         start=True, stop=True)
                last.then_inc(s_scA, 1)
                pe.wait_ge(s_lvB, hd + 1)
                for b in range(TB):
                    tok = slice(b * P, (b + 1) * P)
                    for l in range(3, 7):
                        last = pe.matmul(ps[6 + b][:, (l - 3) * P:(l - 2) * P], ks[:, l, tok], qp[:, l, tok],
                                         start=True, stop=True)
                last.then_inc(s_scB, 1)
                pe.wait_ge(s_lvC, hd + 1)
                pe.wait_ge(s_mA, hd + 1)
                pe.matmul(ps[4][:, 0:P], ks[:, 7, 0:P], qp[:, 7, P:SEQ], start=True, stop=True).then_inc(s_cross, 1)
                pe.wait_ge(s_hv, hd + 1)
                pe.wait_ge(s_orstd, hd + 1)
                pe.wait_ge(s_m0, hd + 1)
                for l in range(LEVELS):
                    pe.matmul(ps[3][:, 0:P], hv[:, 0, :], msk[:, 0, l, :], start=(l == 0), stop=(l == LEVELS - 1))
                pe.wait_ge(s_crossC, hd + 1)
                pe.matmul(ps[3][:, P:SEQ], hv[:, 0, :], aT[:], start=True, stop=False)
                pe.wait_ge(s_mB, hd + 1)
                for l in range(LEVELS):
                    last = pe.matmul(ps[3][:, P:SEQ], hv[:, 1, :], msk[:, 1, l, :], start=False, stop=(l == LEVELS - 1))
                last.then_inc(s_oT, 1)
                pe.wait_ge(s_pn0, hd + 1)
                pe.wait_ge(s_pn, hd + 1)
                for t in range(3):
                    last = pe.transpose(ps[1][:, t * P:(t + 1) * P], prob[:, t * P:(t + 1) * P], ident[:])
                last.then_inc(s_pT, 1)
                pe.wait_ge(s_osq, hd + 1)
                pe.matmul(ps[3][:, SEQ:2 * SEQ], ones[:], osq[:], start=True, stop=True).then_inc(s_oss, 1)
                pe.wait_ge(s_pTc, hd + 1)
                pe.wait_ge(s_avh, hd + 1)
                pe.wait_ge(s_aoc, hd + 1)
                pe.matmul(ps[2][:, 0:SEQ], avh[:, 0, :], probT[:, 0:SEQ], start=True, stop=False, skip_group_check=True)
                pe.matmul(ps[2][:, P:SEQ], avh[:, 1, :], probT[:, SEQ:], start=False, stop=True,
                          skip_group_check=True).then_inc(s_ao, 1)

            def mod_row(a, banks):
                for q in range(4):
                    last = pe.matmul(ps[banks[q]][:, :], ones[:], a[:, q * UW:(q + 1) * UW], start=True, stop=True)
                last.then_inc(s_red, 1)

            pe.wait_ge(s_ada, PH["av"].ada0 + 4)
            mod_row(acc, (4, 5, 6, 7))
            pe.wait_ge(s_aoc, HEADS + 1)
            with pe.Fori(0, PH["out"].groups // 2) as turn:
                for ph in (PH["out"], Group(PH["out"], 1)):
                    token_group(ph, turn * 2, h_hi, h_lo, bank0=ph.tile0 % 4, reuse=4,
                                ready=lambda j: (1, 1, 2, 3)[j // 2], ready_sem=s_mix)

            pe.wait_ge(s_xn, 2)
            pe.wait_ge(s_redc, 8)
            x_transposes(xn, 1, 0, 4)
            ph = PH["up"]
            channel_group(ph, 0, KT, 0, 8, between=lambda j: x_transposes(xn, 1, 4 + 2 * j, 6 + 2 * j) if j < 2 else None)
            channel_group(Group(ph, 1), 0, KT, 4, 8)
            with pe.Fori(1, ph.groups // 2) as i:
                for half in range(2):
                    pe_group = Group(ph, half)
                    channel_group(pe_group, i * 2, KT, 4 * half, 8)
            pe.wait_ge(s_ada, PH["down"].ada0 + 4)
            pe.wait_ge(s_evac, PH["down"].tile0 - 4 + 4)
            mod_row(acc_g2, (0, 1, 2, 3))
            ph = PH["down"]
            for g in range(ph.groups):
                if g == 2:
                    pe.wait_ge(s_redc, 9)
                token_group(ph, g, lambda k, b: act_hi[:, k, b * P:(b + 1) * P], lambda k, b: act_lo[:, k, b * P:(b + 1) * P],
                            ph.unit0 + g * ph.units, (4, 6, 0, 2)[g], 2 if g == 0 else 6,
                            lambda j: 2 * KT + (UK * j) // 4 + 1)

        @block.vector
        def _(dve):
            st = Steps(dve, s_v)
            for start in (s_smask, s_rotU):
                dve.sem_inc(start, 1)
            dve.sem_inc(s_convu, 1)
            dve.sem_inc(s_lo, RING)
            dve.sem_inc(s_ada, RING)
            dve.sem_inc(s_evac, 4)

            dve.wait_ge(s_prmT, 1)
            dve.tensor_copy(prm[:, 0:65], ps[0][:, 0:65]).then_inc(s_prm, 1)
            dve.wait_ge(s_prm, 1)
            st.then(dve.tensor_tensor(lbm, lbl[:, 0:8], lbl[:, 8:16], ALU.max))
            st.do(dve.tensor_tensor(lbe[:, 0:8], lbl[:, 0:8], lbm, ALU.subtract))
            dve.tensor_tensor(lbe[:, 8:16], lbl[:, 8:16], lbm, ALU.subtract).then_inc(s_lbd, 1)
            dve.wait_ge(s_lbe, 1)
            st.then(dve.tensor_tensor(lbm, lbe[:, 0:8], lbe[:, 8:16], ALU.add))
            st.then(dve.reciprocal(lbm, lbm))
            st.then(dve.tensor_tensor(lb, lbe[:, 0:8], lbm, ALU.mult))
            st.then(dve.tensor_scalar(one_lb, lb, -1.0, 1.0, ALU.mult, ALU.add))

            def x_normed(dst, src, n):
                dve.wait_ge(s_rt, n + 1)
                st.then(dve.reciprocal(ss, rstd))
                st.do(dve.tensor_scalar(dst[:, 0, :], src[:, 0, :], ss[:, 0:1], None, ALU.mult))
                dve.wait_ge(s_v, st.n)
                return dve.tensor_scalar(dst[:, 1, :], src[:, 1, :], ss[:, 1:2], None, ALU.mult)

            dve.wait_ge(s_acc, 32)
            dve.wait_ge(s_csilu, 1)

            def first_sums(r0, r1):
                with dve.Fori(r0, r1) as r:
                    for n in range(4):
                        a = (acc, acc_b)[n % 2]
                        dve.wait_ge(s_as[n], r * 16 + 16)
                        dve.wait_ge(s_ada, r * 4 + (n - 1 + 4))
                        dve.scalar_tensor_tensor(out=a[:], in0=astart[:, n], scalar=csilu[:, bass.ds(r * 2 + n // 2, 1)],
                                                 in1=a[:], op0=ALU.mult, op1=ALU.add).then_inc(s_ada, 1)

            first_sums(0, 2)
            x_normed(x0, x0, 0).then_inc(s_xn, 1)

            posf, ang, turns, wrap = rtmp[0:ROT, 0, :], sinr[0:ROT], cosr[0:ROT], rtmp[0:ROT, 1, :]
            MAGIC = 1.5 * 2 ** 23
            T1 = 6.28125
            T2 = float(np.float32(np.round((2 * np.pi - T1) * 2 ** 20) / 2 ** 20))
            T3 = 2 * np.pi - T1 - T2
            dve.wait_ge(s_in, 7 * 16)
            st.then(dve.tensor_copy(wrap, posf.bitcast(I32)))
            st.then(dve.tensor_scalar(ang, wrap, freq[0:ROT], None, ALU.mult))
            st.then(dve.tensor_scalar(turns, ang, 1.0 / (2 * np.pi), MAGIC, ALU.mult, ALU.add))
            st.then(dve.tensor_scalar(turns, turns, -MAGIC, None, ALU.add))
            for part in (T1, T2, T3):
                st.then(dve.scalar_tensor_tensor(out=ang, in0=turns, scalar=-part, in1=ang, op0=ALU.mult, op1=ALU.add))
            PI = float(np.float32(3.1415925))
            st.then(dve.tensor_scalar(ang, ang, PI, -PI, ALU.min, ALU.max))
            st.then(dve.tensor_scalar(turns, ang, np.pi / 2, None, ALU.add))
            st.then(dve.tensor_scalar(wrap, turns, PI, -2 * np.pi, ALU.is_gt, ALU.mult))
            st.then(dve.tensor_tensor(turns, turns, wrap, ALU.add))
            dve.tensor_scalar(turns, turns, PI, -PI, ALU.min, ALU.max).then_inc(s_ang, 1)

            dve.wait_ge(s_prmT, 2)
            dve.tensor_copy(prm[:, 65:], ps[0][:, 65:NPRM]).then_inc(s_prm, 1)
            first_sums(2, KT // 2)

            def ada(a, mine, slot, count, row, half):
                dve.wait_ge(s_a[slot], count)
                dve.wait_ge(s_ada, mine)
                cols = slice(half * AW, (half + 1) * AW)
                dve.scalar_tensor_tensor(out=a[:, cols], in0=araw[:, slot], scalar=csilu[:, bass.ds(row, 1)],
                                         in1=a[:, cols], op0=ALU.mult, op1=ALU.add).then_inc(s_ada, 1)

            def first_columns(q):
                cols = slice(4 * q, 4 * q + 4)
                dve.wait_ge(s_red, 2 * q + 2)
                st.do(dve.tensor_copy(B1[:, cols], ps[4 + q][:, 4 * q:4 * q + 4]))
                dve.scalar_tensor_tensor(out=A1[:, cols], in0=ps[4 + q][:, KT + 4 * q:KT + 4 * q + 4], scalar=1.0,
                                         in1=n1w[:, cols], op0=ALU.add, op1=ALU.mult).then_inc(s_redc, 1)
                dve.wait_ge(s_redc, q + 1)
                st.wait()

            def h_tiles(n, src, scale, shift, ready=None):
                for k in range(KT + 1):
                    if n == 0 and k < KT and k % 4 == 0:
                        first_columns(k // 4)
                    if k < KT:
                        if ready:
                            dve.wait_ge(s_xT, ready(k))
                        if k >= 2:
                            dve.wait_ge(s_h, n * KT + k - 1)
                        dve.tensor_scalar(htmp[:, k % 2], src(k), scale[:, k:k + 1], shift[:, k:k + 1],
                                          ALU.mult, ALU.add).then_inc(s_ht, 1)
                    if k >= 1:
                        dve.wait_ge(s_hhi, n * KT + k)
                        dve.tensor_tensor(h[:, k - 1, 1, :], htmp[:, (k - 1) % 2], h[:, k - 1, 0, :].bitcast(F32),
                                          ALU.subtract).then_inc(s_h, 1)
                    if n == 0 and k >= 2 and k % 2 == 0 and k // 2 <= AHEAD:
                        j = k // 2 - 1
                        dve.wait_ge(s_hi, j + 1)
                        dve.tensor_tensor(wlo[:, j], wraw[:, j], whi[:, j].bitcast(F32), ALU.subtract).then_inc(s_lo, 1)

            dve.wait_ge(s_xTc, KT // 2)
            h_tiles(0, lambda k: xT[:, k, :], A1, B1)

            def lo_part(unit, slot, ready):
                dve.wait_ge(s_hi, unit)
                dve.wait_ge(s_pe, ready)
                dve.tensor_tensor(wlo[:, slot], wraw[:, slot], whi[:, slot].bitcast(F32), ALU.subtract).then_inc(s_lo, 1)

            def stream(name, acc_of=None, row0=0, tiles_at=0, cols_at=0, between=None):
                with dve.Fori(0, PH[name].groups // 2) as turn:
                    i = turn * 2
                    for g, ph in enumerate((PH[name], Group(PH[name], 1))):
                        pe0 = i * ph.pe_per + ph.pe0
                        n, bank0 = ph.units, ph.tile0 % 8
                        for j in range(AHEAD, n + AHEAD):
                            if j == n + AHEAD - 1:
                                for t in range(0, ph.tiles, 2):
                                    if ph.kind == "channel":
                                        dve.wait_ge(s_evt, i * 2 + (ph.chan0 // 2 + t // 2 + 1))
                                        dve.tensor_tensor(proj[:, bass.ds(i * 4 + (tiles_at + 4 * g + t), 2), :],
                                                          bank[:, bank0 + t:bank0 + t + 2, 0:SEQ],
                                                          evt[:, t:t + 2], ALU.add).then_inc(s_evac, 2)
                                    else:
                                        for b in range(TB):
                                            dve.wait_ge(s_pe, pe0 + (n - 1 + b + 1))
                                            dve.tensor_copy(vtok[:, b, bass.ds(i * UW + (cols_at + g * UW), UW)],
                                                            ps[bank0 + b]).then_inc(s_evac, 1)
                            lo_part(i * n + (ph.unit0 + j + 1), j % RING, slot_free(ph, pe0, j))
                            if between:
                                between(g, j)
                            if ph.ada:
                                a = j - AHEAD
                                ada(acc_of, i * 8 + (ph.ada0 + a - 1 + 4), a % RING,
                                    i * 32 + ((ph.ada0 - 2 * KT + a) // RING + 1) * 16, i * 4 + (row0 + 4 * g + a // 2), a % 2)

            dve.wait_ge(s_acc, 48)
            stream("hq_hf", acc, 0, HQ)
            dve.wait_ge(s_acc_c, 16)

            def shift2(g, j):
                if g == 1 and j == AHEAD + 2:
                    dve.wait_ge(s_red, 9)
                    dve.tensor_copy(B2, ps[7][:, 0:KT]).then_inc(s_redc, 1)

            stream("hi", acc_c, 0, 0, 0, shift2)
            stream("hg", acc_c, 8, HG)
            dve.wait_ge(s_acc, 64)
            dve.wait_ge(s_redc, 5)
            stream("aq_ak", acc, 0, AQ)
            dve.wait_ge(s_gates, 2)
            for hd in range(HEADS):
                st.do(dve.tensor_scalar(proj[:, HF + hd, :], proj[:, HF + hd, :], one_lb[:, hd:hd + 1], lb[:, hd:hd + 1],
                                        ALU.mult, ALU.add))
            qv = proj[:, HQ:HQ + 8, :]
            dve.tensor_scalar(qv, qv, SCALE, None, ALU.mult).then_inc(s_f, 1)
            dve.wait_ge(s_f, 1)
            st.wait()

            def rope(part, step):
                heads = proj[0:ROT, (AQ, AK)[part]:(AQ, AK)[part] + 8, :]
                if step == 0:
                    dve.wait_ge(s_cs, 2)
                    dve.wait_ge(s_rotP, part + 1)
                    dve.tensor_tensor(rtmp8[0:ROT], bank[0:ROT, 0:4, :].rearrange("p b (a t) -> p (b a) t", a=2),
                                      sinr[0:ROT].unsqueeze(1).to_broadcast([ROT, 8, SEQ]), ALU.mult).then_inc(s_rotU, 1)
                elif step == 1:
                    st.do(dve.tensor_tensor(heads, heads, cosr[0:ROT].unsqueeze(1).to_broadcast([ROT, 8, SEQ]), ALU.mult))
                else:
                    dve.wait_ge(s_rotU, part + 2)
                    st.wait()
                    dve.tensor_tensor(heads, heads, rtmp8[0:ROT], ALU.add).then_inc(s_rope if part else s_rope0, 1)

            stream("av", None, 0, 0, HEADS * DH,
                   lambda g, j: rope(0, j - AHEAD - 2) if g == 1 and AHEAD + 2 <= j < AHEAD + 5 else None)
            dve.wait_ge(s_rope0, 1)
            for step in range(3):
                rope(1, step)
            dve.wait_ge(s_red, 10)
            dve.scalar_tensor_tensor(out=A2, in0=ps[4][:, KT:2 * KT], scalar=1.0, in1=n2w, op0=ALU.add,
                                     op1=ALU.mult).then_inc(s_redc, 1)
            dve.wait_ge(s_redc, 6)
            dve.wait_ge(s_lvm, 1)
            with dve.Fori(0, HEADS) as hd:
                st.enter(hd, 40)
                f_h = proj[:, bass.ds(hd + HF, 1), :].rearrange("p a t -> p (a t)")
                q_h = proj[:, bass.ds(hd + HQ, 1), :].rearrange("p a t -> p (a t)")
                dve.wait_ge(s_cross, hd + 1)
                st.do(dve.tensor_scalar(ks[:, 0], f_h, -1.0, 1.0, ALU.mult, ALU.add))
                st.then(dve.tensor_tensor(qp[:, 0], q_h, f_h, ALU.mult))
                seg = f_h
                lv_sems = {3: s_lvA, 7: s_lvB}
                off = 0
                for l in range(LEVELS - 1):
                    w = 1 << l
                    n = SEQ // (2 * w)

                    def halves(a):
                        return a.rearrange("p (n two w) -> p n two w", two=2, w=w)

                    segs = seg.rearrange("p (n two) -> p n two", two=2)
                    first, second = segs[:, :, 0:1], segs[:, :, 1:2]
                    ql, qn, kl, kn = halves(qp[:, l]), halves(qp[:, l + 1]), halves(ks[:, l]), halves(ks[:, l + 1])
                    st.do(dve.tensor_copy(qn[:, :, 0], ql[:, :, 0]))
                    st.do(dve.tensor_copy(kn[:, :, 1], kl[:, :, 1]))
                    st.do(dve.tensor_tensor(qn[:, :, 1], ql[:, :, 1], first.to_broadcast([P, n, w]), ALU.mult))
                    if l < LEVELS - 2:
                        nxt = tot[:, off:off + n]
                        st.do(dve.tensor_tensor(nxt.unsqueeze(2), first, second, ALU.mult))
                        off += n
                        seg = nxt
                    ins = dve.tensor_tensor(kn[:, :, 0], kl[:, :, 0], second.to_broadcast([P, n, w]), ALU.mult)
                    if l == 1:
                        ins.then_inc(s_lvA, 1)
                        dve.wait_ge(s_lvA, hd + 1)
                        st.wait()
                    elif l == 5:
                        ins.then_inc(s_lvB, 1)
                        dve.wait_ge(s_lvB, hd + 1)
                        st.wait()
                    elif l == 6:
                        ins.then_inc(s_lvC, 1)
                    else:
                        st.then(ins)
                dve.wait_ge(s_S, hd + 1)
                dve.wait_ge(s_pT, hd + 1)
                dve.tensor_tensor(smask[:], ps[0][:, 0:3 * P], neg, ALU.add).then_inc(s_smask, 1)
                dve.wait_ge(s_smask, hd + 2)
                st.do(dve.tensor_reduce(mx[:, 0:1], smask[:, 0:P], AX.X, ALU.max))
                st.then(dve.tensor_reduce(mx[:, 1:2], smask[:, P:], AX.X, ALU.max))
                dve.tensor_scalar(mx, mx, -SCALE, None, ALU.mult).then_inc(s_smax, 1)
                dve.wait_ge(s_scA, hd + 1)
                dve.wait_ge(s_scB, hd + 1)
                for b in range(TB):
                    for part, freed in ((0, s_mA), (1, s_mB)):
                        lv = slice(4 * part, 4 * part + 4)
                        ins = dve.tensor_tensor(msk[:, b, lv, :], ps[4 + 2 * part + b][:, :].rearrange("p (l t) -> p l t", l=4),
                                                lvm[:, lv, :], ALU.mult)
                        if b:
                            ins.then_inc(freed, 1)
                        elif part:
                            ins.then_inc(s_m0, 1)
                        else:
                            st.do(ins)
                dve.wait_ge(s_prob, hd * 2 + 2)
                st.then(dve.tensor_tensor(prob[:], prob[:], mult, ALU.mult))
                st.do(dve.tensor_reduce(den[:, 0:1], prob[:, 0:P], AX.X, ALU.add))
                st.then(dve.tensor_reduce(den[:, 1:2], prob[:, P:], AX.X, ALU.add))
                st.then(dve.reciprocal(rden, den))
                dve.tensor_scalar(prob[:, 0:P], prob[:, 0:P], rden[:, 0:1], None, ALU.mult).then_inc(s_pn0, 1)
                dve.tensor_scalar(prob[:, P:], prob[:, P:], rden[:, 1:2], None, ALU.mult).then_inc(s_pn, 1)
            st.leave(HEADS)

            dve.wait_ge(s_mixhi, 1)
            dve.tensor_tensor(h[:, 0:8, 1, :], proj[:, AQ:AQ + 8, :], h[:, 0:8, 0, :].bitcast(F32), ALU.subtract).then_inc(s_mix, 1)
            rv = proj[:, HF:HF + 8, :]
            dve.wait_ge(s_orstd, HEADS + 1)
            dve.wait_ge(s_oc, HEADS)
            dve.wait_ge(s_gates, 3)
            st.then(dve.reciprocal(rv, rv))
            for half in range(2):
                ov, rv, gv = (proj[:, a + 4 * half:a + 4 * half + 4, :] for a in (HQ, HF, HG))
                st.then(dve.tensor_tensor(ov, ov, rv, ALU.mult))
                dve.scalar_tensor_tensor(out=gv, in0=ov, scalar=gn, in1=gv, op0=ALU.mult, op1=ALU.mult).then_inc(s_hdone, 1)
            dve.wait_ge(s_red, 11)
            for q in range(4):
                ins = dve.tensor_copy(g1b[:, q * UW:(q + 1) * UW], ps[4 + q][:, :])
                if q < 3:
                    st.do(ins)
            ins.then_inc(s_redc, 2)
            for half in range(2):
                tiles = slice(8 + 4 * half, 12 + 4 * half)
                dve.wait_ge(s_mixhi, 2 + half)
                dve.tensor_tensor(h[:, tiles, 1, :], proj[:, HG + 4 * half:HG + 4 * half + 4, :],
                                  h[:, tiles, 0, :].bitcast(F32), ALU.subtract).then_inc(s_mix, 1)
            dve.wait_ge(s_redc, 8)
            st.wait()

            ph = PH["out"]
            with dve.Fori(0, ph.groups // 2) as turn:
                st.enter(turn, 4)
                i = turn * 2
                for g, ph in enumerate((PH["out"], Group(PH["out"], 1))):
                    pe0 = i * ph.pe_per + ph.pe0
                    for j in range(AHEAD, 8 + AHEAD):
                        lo_part(i * 8 + (ph.unit0 + j + 1), j % RING, slot_free(ph, pe0, j))
                    dve.wait_ge(s_xre, 16)
                    for b in range(TB):
                        cols = bass.ds(i * UW + g * UW, UW)
                        dve.wait_ge(s_pe, pe0 + (7 + b + 1))
                        st.wait()
                        dve.tensor_tensor(ytmp[:], ps[ph.tile0 % 4 + b][:, :], g1b[:, cols], ALU.mult).then_inc(s_evac, 1)
                        dve.wait_ge(s_evac, i * 2 + (ph.tile0 + b + 1 + 4))
                        st.do(dve.tensor_tensor(x1[:, b, cols], x1[:, b, cols], ytmp[:], ALU.add))
            st.leave(PH["out"].groups // 2)
            st.wait()
            dve.sem_inc(s_ms, 1)
            x_normed(xn, x1, 1).then_inc(s_xn, 1)
            h_tiles(1, lambda k: ps[4 + (k // 2) % 4][:, (k % 2) * SEQ:(k % 2 + 1) * SEQ], A2, B2,
                    lambda k: KT // 2 + k // 2 + 1)

            ph = PH["up"]
            chan_groups = ph.chan0 // 4 * 2

            def conv_step(i, half, step):
                dst = up if half else gate

                def w(tap, f):
                    return cw[:, bass.ds(i * 4 + (half * NF + tap * 88 + f), 1)]

                if step == 0:
                    dve.wait_ge(s_evt, i * 2 + (chan_groups + half + 1))
                    dve.tensor_tensor(evt[:], bank[:, 4 * half:4 * half + 4, 0:SEQ], evt[:], ALU.add).then_inc(s_evac, 4)
                elif step == 1:
                    dve.wait_ge(s_evac, i * 8 + (ph.tile0 + 4 * half + 4 + 4))
                    for f in range(4):
                        st.do(dve.tensor_scalar(dst[:, f, :], evt[:, f, :], w(2, f), cb[:, bass.ds(i * 4 + (half * NF + f), 1)],
                                                ALU.mult, ALU.add))
                elif step == 2:
                    st.wait()
                    for f in range(4):
                        st.do(dve.scalar_tensor_tensor(out=dst[:, f, 1:], in0=evt[:, f, :SEQ - 1], scalar=w(1, f),
                                                       in1=dst[:, f, 1:], op0=ALU.mult, op1=ALU.add))
                elif step == 3:
                    st.wait()
                    for f in range(4):
                        ins = dve.scalar_tensor_tensor(out=dst[:, f, 2:], in0=evt[:, f, :SEQ - 2], scalar=w(0, f),
                                                       in1=dst[:, f, 2:], op0=ALU.mult, op1=ALU.add)
                        if f == 3:
                            ins.then_inc(s_convu if half else s_convg, 1)
                        else:
                            st.do(ins)
                elif step == 4 and half:
                    st.wait()
                    dve.wait_ge(s_convu, i + 2)
                    dve.wait_ge(s_silu, i + 1)
                    dve.tensor_tensor(up[:], up[:], gate[:], ALU.mult).then_inc(s_prod, 1)
                elif step == 6 and half:
                    dve.wait_ge(s_acthi, i + 1)
                    dve.wait_ge(s_prod, i + 1)
                    tiles = bass.ds(i * 4, 4)
                    dve.tensor_tensor(act_lo[:, tiles, :], up[:], act_hi[:, tiles, :].bitcast(F32), ALU.subtract).then_inc(s_h, 1)

            def ffn_half(i, half, finished, with_ada):
                pe0 = (i * 2 + half) * ph.pe_per + ph.pe0
                for j in range(AHEAD, 8 + AHEAD):
                    lo_part(i * 16 + (ph.unit0 + half * 8 + j + 1), j % RING, slot_free(ph, pe0, j))
                    if finished:
                        conv_step(i if half else i - 1, 1 - half, j - AHEAD)
                    if with_ada and j % 4 == 1:
                        if not finished:
                            dve.wait_ge(s_acc, 80)
                        n = half * 2 + (j - AHEAD) // 4
                        ada(acc_g2, i * 4 + (ph.ada0 + n - 1 + 4), n, i * 16 + ((ph.ada0 - 2 * KT) // RING + 1) * 16,
                            i * 2 + n // 2, n % 2)

            def pair(i, finished, with_ada):
                ffn_half(i, 0, finished, with_ada)
                ffn_half(i, 1, True, with_ada)

            PER = 22
            pair(0, False, True)
            dve.wait_ge(s_spill, 16)
            with dve.Fori(1, ph.ada_pairs) as i:
                st.enter(i - 1, PER)
                pair(i, True, True)
            st.leave(ph.ada_pairs - 1)
            with dve.Fori(ph.ada_pairs, ph.groups // 2) as i:
                st.enter(i - ph.ada_pairs, PER)
                pair(i, True, False)
            st.leave(ph.groups // 2 - ph.ada_pairs)

            last = ph.groups // 2 - 1
            ph_down = PH["down"]
            for g in range(ph_down.groups):
                pe0 = ph_down.pe0 + g * ph_down.pe_per
                for j in range(AHEAD, ph_down.units + AHEAD):
                    if g == 0 and j == AHEAD:
                        conv_step(last, 1, 0)
                    unit = ph_down.unit0 + g * ph_down.units + j
                    if unit < ph_down.unit0 + ph_down.groups * ph_down.units:
                        lo_part(unit + 1, unit % RING, slot_free(ph_down, pe0, j))
                    if g == 0 and AHEAD < j < AHEAD + 7:
                        conv_step(last, 1, j - AHEAD)
                    if g == 0 and AHEAD + 9 <= j < AHEAD + 13:
                        q = j - AHEAD - 9
                        dve.wait_ge(s_red, 12)
                        ins = dve.tensor_copy(g2b[:, q * UW:(q + 1) * UW], ps[q])
                        if q < 3:
                            st.do(ins)
                        else:
                            ins.then_inc(s_redc, 1)
                if g == 0:
                    dve.wait_ge(s_xr, 32)
                    dve.wait_ge(s_redc, 9)
                for b in range(TB):
                    cols = slice(g * UW, (g + 1) * UW)
                    dve.wait_ge(s_pe, pe0 + ph_down.units - 1 + b + 1)
                    st.wait()
                    dve.tensor_tensor(junk2[:, 0:UW], ps[(4, 6, 0, 2)[g] + b], g2b[:, cols], ALU.mult).then_inc(s_evac, 1)
                    dve.wait_ge(s_evac, ph_down.tile0 + g * 2 + b + 1 + 4)
                    st.do(dve.tensor_tensor(xr[:, b, cols], xr[:, b, cols], junk2[:, 0:UW], ALU.add))
            st.wait()
            dve.sem_inc(s_ms, 1)
            dve.wait_ge(s_rt, 3)
            st.then(dve.reciprocal(ss, rstd))
            for b in range(TB):
                for part in range(2):
                    cols = slice(part * AW, (part + 1) * AW)
                    dve.scalar_tensor_tensor(out=xr[:, b, cols], in0=xr[:, b, cols], scalar=ss[:, b:b + 1], in1=fnb[:, cols],
                                             op0=ALU.mult, op1=ALU.mult).then_inc(s_fin, 1)


_INS = ["x", "c", "positions", "w_ada", "b_ada", "norm1_w", "w_in", "lb_logits", "gnorm_w", "w_out",
        "norm2_w", "w_up", "conv_w", "conv_b", "w_down", "final_norm_w"]


def kernel(**inputs):
    import numpy as _np
    import concourse.bacc as _bacc
    from concourse import mybir as _mybir
    from concourse.bass_utils import run_bass_kernel_spmd as _run

    nc = _bacc.Bacc("TRN2", target_bir_lowering=False, num_devices=1)
    arrays, args = {}, []
    f32, lv = constants()
    for name, a in [(n, _np.ascontiguousarray(inputs[n])) for n in _INS] + [("tab_f32", f32), ("tab_lv", lv)]:
        arrays[f"in_{name}"] = a
        args.append(nc.dram_tensor(f"in_{name}", a.shape, _mybir.dt.from_np(a.dtype), kind="ExternalInput").ap())
    args.append(nc.dram_tensor("out_0", (1, SEQ, D), _mybir.dt.float32, kind="ExternalOutput").ap())
    build(nc, *args)
    r = _run(nc, [arrays], core_ids=[0])
    return r.results[0]["out_0"]
```
